# Optimizing a Trainium2 kernel written in Bass

```python
import numpy as np
import jax
import jax.numpy as jnp
from jax import lax

D_MODEL = 1024
BATCH = 1
SEQ = 256
DEPTH = 2

H_A = 4
DH_NOPE = 64
DH_ROPE = 32
D_C = 128
DH_V = 64
H_I = 4
D_I = 64
K_SEL_MAX = 256
ROPE_THETA = 10000.0
H_B = 4
DH_B = 128
CONV_W = 4
CHUNK = 64
F_BIAS_LO = 3.0
F_BIAS_HI = 6.0
H_C = 4
DH_C = 64
L_CMP = 32
D_STRIDE = 16
CMP_HIDDEN = 128
L_SEL = 64
N_TOP_MAX = 16
WINDOW = 512
Q_BLOCK = 128
D_FF = 2816
N_EXPERTS = 8
TOP_K_EXPERTS = 2
D_FF_EXPERT = 3584
N_DENSE = (DEPTH + 1) // 2
N_MOE = DEPTH // 2
N_MOD = 6
ALPHA = (2 * DEPTH) ** 0.25
BETA = (8 * DEPTH) ** -0.25
MIX_OUT = H_A * DH_V + H_B * DH_B + H_C * DH_C
SPLIT_SIZES = (H_A * DH_NOPE, H_A * DH_ROPE, D_C, DH_ROPE, H_I * D_I, D_I, H_I, H_B * DH_B, H_B * DH_B, H_B * DH_B, H_B, H_B, H_B * DH_B, H_C * DH_C, DH_C, DH_C, DH_C, DH_C, DH_C, DH_C, 3 * H_C)
P_IN = sum(SPLIT_SIZES)

kernel_name = 'hybrid_dsa_mlstm_nsa_moe_block'

def _layer_norm(x, g, b, eps=1e-5):
    xf = x.astype(jnp.float32)
    mu = jnp.mean(xf, -1, keepdims=True)
    var = jnp.mean(jnp.square(xf - mu), -1, keepdims=True)
    return ((xf - mu) * lax.rsqrt(var + eps) * g + b).astype(x.dtype)

def _rms_norm(x, g, eps=1e-6):
    xf = x.astype(jnp.float32)
    return (xf * lax.rsqrt(jnp.mean(xf * xf, -1, keepdims=True) + eps) * g).astype(x.dtype)

def _masked_softmax(s, mask):
    s = jnp.where(mask, s.astype(jnp.float32), -jnp.inf)
    m = jnp.max(s, axis=-1, keepdims=True)
    m = jnp.where(jnp.isfinite(m), m, 0.0)
    e = jnp.where(mask, jnp.exp(s - m), 0.0)
    return e / jnp.maximum(jnp.sum(e, axis=-1, keepdims=True), 1e-30)

def _rope(x, ang):
    x1, x2 = jnp.split(x.astype(jnp.float32), 2, axis=-1)
    cos, sin = jnp.cos(ang), jnp.sin(ang)
    return jnp.concatenate([x1 * cos - x2 * sin, x1 * sin + x2 * cos], -1).astype(x.dtype)

def _gather_rows(table, idx):
    return jax.vmap(lambda t, i: t[i])(table, idx)

def _to_blocks(a):
    return a.reshape(a.shape[0], -1, Q_BLOCK, *a.shape[2:]).swapaxes(0, 1)

def _from_blocks(a):
    a = a.swapaxes(0, 1)
    return a.reshape(a.shape[0], -1, *a.shape[3:])

def _block_starts(seq):
    return jnp.arange(seq // Q_BLOCK, dtype=jnp.int32) * Q_BLOCK

def _dsa_group(q_nope, q_rope, ckv, k_rope, iq, ik, iw, positions, w_uk, w_uv, kv_norm):
    bsz, seq = q_nope.shape[:2]
    k_sel = min(K_SEL_MAX, seq // 4)
    scale = (DH_NOPE + DH_ROPE) ** -0.5
    inv_freq = ROPE_THETA ** (-jnp.arange(0, DH_ROPE, 2, dtype=jnp.float32) / DH_ROPE)
    ang = positions.astype(jnp.float32)[..., None] * inv_freq
    q_rope = _rope(q_rope.reshape(bsz, seq, H_A, DH_ROPE), ang[:, :, None, :])
    k_rope = _rope(k_rope, ang)
    ckv = _rms_norm(ckv, kv_norm)
    q_abs = jnp.einsum('bshd,hdc->bshc', q_nope.reshape(bsz, seq, H_A, DH_NOPE), w_uk)
    iq = iq.reshape(bsz, seq, H_I, D_I)
    key_pos = jnp.arange(seq)

    def block(args):
        qa, qr, iqb, iwb, t0 = args
        q_pos = t0 + jnp.arange(Q_BLOCK)
        causal = key_pos[None, :] <= q_pos[:, None]
        logits = jnp.einsum('bthd,bsd->bths', iqb, ik)
        score = jnp.einsum('bths,bth->bts', jax.nn.relu(logits), iwb)
        score = jnp.where(causal[None], score, -jnp.inf)
        top_val, top_idx = lax.top_k(score, k_sel)
        valid = top_val > -jnp.inf
        c_sel = _gather_rows(ckv, top_idx)
        r_sel = _gather_rows(k_rope, top_idx)
        s = (jnp.einsum('bthc,btkc->bthk', qa, c_sel) + jnp.einsum('bthr,btkr->bthk', qr, r_sel)) * scale
        p = _masked_softmax(s, valid[:, :, None, :]).astype(c_sel.dtype)
        o_lat = jnp.einsum('bthk,btkc->bthc', p, c_sel)
        return jnp.einsum('bthc,hcd->bthd', o_lat, w_uv)

    out = lax.map(block, (_to_blocks(q_abs), _to_blocks(q_rope), _to_blocks(iq), _to_blocks(iw), _block_starts(seq)))
    return _from_blocks(out)

def _causal_conv(x, w, b):
    y = lax.conv_general_dilated(x, w[:, None, :].astype(x.dtype), (1,), [(CONV_W - 1, 0)], dimension_numbers=('NWC', 'WIO', 'NWC'), feature_group_count=x.shape[-1])
    return y + b

def _mlstm_chunk(state, inp):
    c_mat, n_vec, m = state
    q, k, v, ig, lf = inp
    b = jnp.cumsum(lf, axis=-1)
    tri = jnp.tril(jnp.ones((CHUNK, CHUNK), bool))
    log_d = jnp.where(tri, b[..., :, None] - b[..., None, :] + ig[..., None, :], -jnp.inf)
    log_inter = b + m[..., None]
    m_out = jnp.maximum(log_inter, jnp.max(log_d, -1))
    d = jnp.exp(log_d - m_out[..., None])
    w_inter = jnp.exp(log_inter - m_out)
    s = jnp.einsum('bhjd,bhsd->bhjs', q, k) * d
    num = w_inter[..., None] * jnp.einsum('bhvk,bhjk->bhjv', c_mat, q) + jnp.einsum('bhjs,bhsv->bhjv', s, v)
    den = w_inter * jnp.einsum('bhk,bhjk->bhj', n_vec, q) + jnp.sum(s, -1)
    h = num / jnp.maximum(jnp.abs(den), jnp.exp(-m_out))[..., None]
    b_last = b[..., -1]
    log_w = b_last[..., None] - b + ig
    m_new = jnp.maximum(b_last + m, jnp.max(log_w, -1))
    decay = jnp.exp(b_last + m - m_new)
    w = jnp.exp(log_w - m_new[..., None])
    c_mat = decay[..., None, None] * c_mat + jnp.einsum('bhs,bhsv,bhsk->bhvk', w, v, k)
    n_vec = decay[..., None] * n_vec + jnp.einsum('bhs,bhsk->bhk', w, k)
    return (c_mat, n_vec, m_new), h

def _mlstm_group(q, k, v, i_pre, f_pre, conv_w, conv_b, gate_b):
    bsz, seq = q.shape[:2]
    n_chunk = seq // CHUNK
    f32 = jnp.float32
    qk = jax.nn.silu(_causal_conv(jnp.concatenate([q, k], -1), conv_w, conv_b))
    q_c, k_c = jnp.split(qk, 2, axis=-1)

    def heads(a, scale=1.0):
        a = a.astype(f32).reshape(bsz, n_chunk, CHUNK, H_B, DH_B) * scale
        return a.transpose(1, 0, 3, 2, 4)

    def per_chunk(a):
        return a.reshape(bsz, n_chunk, CHUNK, H_B).transpose(1, 0, 3, 2)

    ig = per_chunk(i_pre.astype(f32) + gate_b[0])
    lf = per_chunk(jax.nn.log_sigmoid(f_pre.astype(f32) + gate_b[1]))
    init = (jnp.zeros((bsz, H_B, DH_B, DH_B), f32), jnp.zeros((bsz, H_B, DH_B), f32), jnp.zeros((bsz, H_B), f32))
    _, h = lax.scan(_mlstm_chunk, init, (heads(q_c), heads(k_c, DH_B ** -0.5), heads(v), ig, lf))
    return h.transpose(1, 0, 3, 2, 4).reshape(bsz, seq, H_B, DH_B).astype(v.dtype)

def _nsa_group(q, k_cmp, v_cmp, k_slc, v_slc, k_win, v_win, g_pre, cmp_pos, cmp_w1, cmp_w2):
    bsz, seq = q.shape[:2]
    scale = DH_C ** -0.5
    q = q.reshape(bsz, seq, H_C, DH_C)
    n_cmp = (seq - L_CMP) // D_STRIDE + 1
    n_sel = seq // L_SEL
    n_top = min(N_TOP_MAX, n_sel)
    cmp_start = np.arange(n_cmp) * D_STRIDE
    cmp_idx = cmp_start[:, None] + np.arange(L_CMP)[None, :]
    sel_start = np.arange(n_sel) * L_SEL
    cover = jnp.asarray(((cmp_start[:, None] < sel_start[None, :] + L_SEL) & (cmp_start[:, None] + L_CMP > sel_start[None, :])).astype(np.float32))
    cmp_end = jnp.asarray(cmp_start + L_CMP - 1)

    def compress(a, j):
        blocks = (a[:, cmp_idx] + cmp_pos[j]).reshape(bsz, n_cmp, L_CMP * DH_C)
        return jax.nn.silu(blocks @ cmp_w1[j]) @ cmp_w2[j]

    kc, vc = compress(k_cmp, 0), compress(v_cmp, 1)
    ks_blk = k_slc.reshape(bsz, n_sel, L_SEL, DH_C)
    vs_blk = v_slc.reshape(bsz, n_sel, L_SEL, DH_C)
    pad = ((0, 0), (WINDOW, 0), (0, 0))
    kw_pad, vw_pad = jnp.pad(k_win, pad), jnp.pad(v_win, pad)
    gates = jax.nn.sigmoid(g_pre.reshape(bsz, seq, 3, H_C))
    blk = jnp.arange(n_sel)
    in_blk = jnp.arange(L_SEL)
    win_off = jnp.arange(WINDOW + Q_BLOCK) - WINDOW

    def block(args):
        qb, gb, t0 = args
        q_pos = t0 + jnp.arange(Q_BLOCK)
        cmask = cmp_end[None, :] <= q_pos[:, None]
        p_c = _masked_softmax(jnp.einsum('bthd,bnd->bthn', qb, kc) * scale, cmask[None, :, None, :])
        o_cmp = jnp.einsum('bthn,bnd->bthd', p_c.astype(vc.dtype), vc)
        imp = jnp.einsum('bthn,nj->btj', p_c, cover)
        cur = q_pos // L_SEL
        admissible = blk[None, :] <= cur[:, None]
        forced = (blk[None, :] == 0) | (blk[None, :] == cur[:, None]) | (blk[None, :] == cur[:, None] - 1)
        imp = jnp.where((admissible & forced)[None], jnp.inf, jnp.where(admissible[None], imp, -jnp.inf))
        top_val, top_idx = lax.top_k(imp, n_top)
        tok_pos = top_idx[..., None] * L_SEL + in_blk
        smask = ((top_val > -jnp.inf)[..., None] & (tok_pos <= q_pos[None, :, None, None])).reshape(bsz, Q_BLOCK, n_top * L_SEL)
        ks = _gather_rows(ks_blk, top_idx).reshape(bsz, Q_BLOCK, n_top * L_SEL, DH_C)
        vs = _gather_rows(vs_blk, top_idx).reshape(bsz, Q_BLOCK, n_top * L_SEL, DH_C)
        p_s = _masked_softmax(jnp.einsum('bthd,btkd->bthk', qb, ks) * scale, smask[:, :, None, :])
        o_slc = jnp.einsum('bthk,btkd->bthd', p_s.astype(vs.dtype), vs)
        kw = lax.dynamic_slice_in_dim(kw_pad, t0, WINDOW + Q_BLOCK, axis=1)
        vw = lax.dynamic_slice_in_dim(vw_pad, t0, WINDOW + Q_BLOCK, axis=1)
        k_pos = t0 + win_off
        wmask = (k_pos[None, :] >= 0) & (k_pos[None, :] <= q_pos[:, None]) & (q_pos[:, None] - k_pos[None, :] < WINDOW)
        p_w = _masked_softmax(jnp.einsum('bthd,bkd->bthk', qb, kw) * scale, wmask[None, :, None, :])
        o_win = jnp.einsum('bthk,bkd->bthd', p_w.astype(vw.dtype), vw)
        return gb[:, :, 0, :, None] * o_cmp + gb[:, :, 1, :, None] * o_slc + gb[:, :, 2, :, None] * o_win

    out = lax.map(block, (_to_blocks(q), _to_blocks(gates), _block_starts(seq)))
    return _from_blocks(out)

def _hybrid_mixer(u, positions, w_in, w_uk, w_uv, kv_norm, conv_w, conv_b, gate_b, cmp_pos, cmp_w1, cmp_w2, grp_norm, w_out):
    bsz, seq = u.shape[:2]
    cuts = np.cumsum(SPLIT_SIZES)[:-1].tolist()
    (qn, qr, ckv, kr, iq, ik, iw, mq, mk, mv, mi, mf, mo, nq, nkc, nvc, nks, nvs, nkw, nvw, ng) = jnp.split(u @ w_in, cuts, axis=-1)
    o_a = _dsa_group(qn, qr, ckv, kr, iq, ik, iw, positions, w_uk, w_uv, kv_norm)
    h_b = _mlstm_group(mq, mk, mv, mi, mf, conv_w, conv_b, gate_b)
    o_c = _nsa_group(nq, nkc, nvc, nks, nvs, nkw, nvw, ng, cmp_pos, cmp_w1, cmp_w2)
    g_a, g_b, g_c = jnp.split(grp_norm, [H_A * DH_V, H_A * DH_V + H_B * DH_B])
    y_a = _rms_norm(o_a, g_a.reshape(H_A, DH_V)).reshape(bsz, seq, -1)
    y_b = _rms_norm(h_b, g_b.reshape(H_B, DH_B)).reshape(bsz, seq, -1) * jax.nn.sigmoid(mo)
    y_c = _rms_norm(o_c, g_c.reshape(H_C, DH_C)).reshape(bsz, seq, -1)
    return jnp.concatenate([y_a, y_b, y_c], -1) @ w_out

def _swiglu(u, w_gate, w_up, w_down):
    return (jax.nn.silu(u @ w_gate) * (u @ w_up)) @ w_down

def _moe_swiglu(u, router, w_gate, w_up, w_down):
    bsz, seq, d = u.shape
    t = u.reshape(-1, d)
    logits = (t @ router).astype(jnp.float32)
    top_val, top_idx = lax.top_k(logits, TOP_K_EXPERTS)
    weights = jax.nn.softmax(top_val, axis=-1)
    combine = jnp.sum(jax.nn.one_hot(top_idx, N_EXPERTS, dtype=jnp.float32) * weights[..., None], axis=1).astype(t.dtype)
    y = jnp.zeros_like(t)
    for e in range(N_EXPERTS):
        y = y + combine[:, e:e + 1] * _swiglu(t, w_gate[e], w_up[e], w_down[e])
    return y.reshape(bsz, seq, d)

def setup_inputs(seed: int = 0) -> dict:
    key = jax.random.key(seed)
    keys = iter(jax.random.split(key, 40))
    f32 = jnp.float32

    def nrm(shape, scale):
        return jax.random.normal(next(keys), shape, f32) * scale

    def gain(shape):
        return 1.0 + nrm(shape, 0.02)

    x = nrm((BATCH, SEQ, D_MODEL), 1.0)
    c = nrm((BATCH, D_MODEL), 1.0)
    positions = jnp.arange(SEQ, dtype=jnp.int32)[None, :] + jax.random.randint(next(keys), (BATCH, 1), 0, SEQ, dtype=jnp.int32)
    f_bias = jnp.linspace(F_BIAS_LO, F_BIAS_HI, H_B, dtype=f32)
    gate_b = jnp.stack([nrm((DEPTH, H_B), 0.1), f_bias + nrm((DEPTH, H_B), 0.1)], axis=1)
    return {
        'x': x,
        'c': c,
        'positions': positions,
        'w_mod': nrm((D_MODEL, DEPTH * N_MOD * D_MODEL), 0.1 * D_MODEL ** -0.5),
        'b_mod': nrm((DEPTH * N_MOD * D_MODEL,), 0.02),
        'w_in': nrm((DEPTH, D_MODEL, P_IN), D_MODEL ** -0.5),
        'dsa_w_uk': nrm((DEPTH, H_A, DH_NOPE, D_C), D_C ** -0.5),
        'dsa_w_uv': nrm((DEPTH, H_A, D_C, DH_V), D_C ** -0.5),
        'dsa_kv_norm': gain((DEPTH, D_C)),
        'mlstm_conv_w': nrm((DEPTH, CONV_W, 2 * H_B * DH_B), CONV_W ** -0.5),
        'mlstm_conv_b': nrm((DEPTH, 2 * H_B * DH_B), 0.02),
        'mlstm_gate_b': gate_b,
        'nsa_cmp_pos': nrm((DEPTH, 2, L_CMP, DH_C), 0.02),
        'nsa_cmp_w1': nrm((DEPTH, 2, L_CMP * DH_C, CMP_HIDDEN), (L_CMP * DH_C) ** -0.5),
        'nsa_cmp_w2': nrm((DEPTH, 2, CMP_HIDDEN, DH_C), CMP_HIDDEN ** -0.5),
        'grp_norm': gain((DEPTH, MIX_OUT)),
        'w_out': nrm((DEPTH, MIX_OUT, D_MODEL), BETA * MIX_OUT ** -0.5),
        'ln_g': gain((DEPTH, 2, D_MODEL)),
        'ln_b': nrm((DEPTH, 2, D_MODEL), 0.02),
        'ffn_w_gate': nrm((N_DENSE, D_MODEL, D_FF), D_MODEL ** -0.5),
        'ffn_w_up': nrm((N_DENSE, D_MODEL, D_FF), D_MODEL ** -0.5),
        'ffn_w_down': nrm((N_DENSE, D_FF, D_MODEL), BETA * D_FF ** -0.5),
        'moe_router': nrm((N_MOE, D_MODEL, N_EXPERTS), D_MODEL ** -0.5),
        'moe_w_gate': nrm((N_MOE, N_EXPERTS, D_MODEL, D_FF_EXPERT), D_MODEL ** -0.5),
        'moe_w_up': nrm((N_MOE, N_EXPERTS, D_MODEL, D_FF_EXPERT), D_MODEL ** -0.5),
        'moe_w_down': nrm((N_MOE, N_EXPERTS, D_FF_EXPERT, D_MODEL), BETA * D_FF_EXPERT ** -0.5),
    }

def reference(x, c, positions, w_mod, b_mod, w_in, dsa_w_uk, dsa_w_uv, dsa_kv_norm, mlstm_conv_w, mlstm_conv_b, mlstm_gate_b, nsa_cmp_pos, nsa_cmp_w1, nsa_cmp_w2, grp_norm, w_out, ln_g, ln_b, ffn_w_gate, ffn_w_up, ffn_w_down, moe_router, moe_w_gate, moe_w_up, moe_w_down):
    bsz = x.shape[0]
    mod = (jax.nn.silu(c) @ w_mod + b_mod).reshape(bsz, DEPTH, N_MOD, D_MODEL)
    for l in range(DEPTH):
        sh1, sc1, g1, sh2, sc2, g2 = [mod[:, l, j, None, :] for j in range(N_MOD)]
        u = x * (1.0 + sc1) + sh1
        y = _hybrid_mixer(u, positions, w_in[l], dsa_w_uk[l], dsa_w_uv[l], dsa_kv_norm[l], mlstm_conv_w[l], mlstm_conv_b[l], mlstm_gate_b[l], nsa_cmp_pos[l], nsa_cmp_w1[l], nsa_cmp_w2[l], grp_norm[l], w_out[l])
        x = _layer_norm(ALPHA * x + (1.0 + g1) * y, ln_g[l, 0], ln_b[l, 0])
        u = x * (1.0 + sc2) + sh2
        if l % 2 == 0:
            y = _swiglu(u, ffn_w_gate[l // 2], ffn_w_up[l // 2], ffn_w_down[l // 2])
        else:
            y = _moe_swiglu(u, moe_router[l // 2], moe_w_gate[l // 2], moe_w_up[l // 2], moe_w_down[l // 2])
        x = _layer_norm(ALPHA * x + (1.0 + g2) * y, ln_g[l, 1], ln_b[l, 1])
    return x


_drawn_inputs = setup_inputs


def setup_inputs(seed=0):
    import zlib

    import numpy as np

    out = dict(_drawn_inputs(seed))
    spreads = {}
    factors = {'dsa_kv_norm': 4.03, 'mlstm_conv_b': 5.005, 'nsa_cmp_pos': 5.008, 'grp_norm': 4.097}
    for name, (base, spread) in spreads.items():
        noise = np.random.default_rng([zlib.crc32(name.encode()), seed]).standard_normal(out[name].shape)
        drawn = base * np.exp(spread * noise) if base else spread * noise
        out[name] = jnp.asarray(drawn.astype(out[name].dtype))
    for name, factor in factors.items():
        out[name] = (out[name] * factor).astype(out[name].dtype)
    return out
```

```python
from contextlib import ExitStack

import numpy as np

import concourse.bass as bass
from concourse import mybir

F32 = mybir.dt.float32
I32 = mybir.dt.int32
U32 = mybir.dt.uint32
ALU = mybir.AluOpType
ACT = mybir.ActivationFunctionType
X = mybir.AxisListType.X

P = 128
D = 1024
T = 256
TILES = T // P
DEPTH = 2
KD = D // P
HEADS = 4
DH_V = 64
D_C = 128
DH_R = 32
DH_B = 128
DH_C = 64
K_SEL = T // 4
N_CMP = (T - 32) // 16 + 1
F_DENSE = 2816
F_EXP = 3584
EXPERTS = 8
ALPHA = (2 * DEPTH) ** 0.25
SCALE_A = (64 + DH_R) ** -0.5
SCALE_B = DH_B ** -0.5
SCALE_C = DH_C ** -0.5
NEG = -1e30
TAKEN = -3e38
TWO_PI = 2.0 * np.pi

RING = 7
SLOT = 3072
MODW = SLOT // KD
FC = 256
C_DENSE = F_DENSE // FC
C_EXP = F_EXP // FC
MOD_SLOTS = 3 * D // MODW
PROJ = [312, 384, 320, 384, 384, 384, 384, 384, 384, 256]
OFF = dict(qn=0, qr=256, ckv=384, kr=512, iq=544, ik=800, iw=864, mq=868, mk=1380, mv=1892, mi=2404,
           mf=2408, mo=2412, nq=2924, nkc=3180, nvc=3244, nks=3308, nvs=3372, nkw=3436, nvw=3500, ng=3564)
PICK = [("qr", 0, 128), ("kr", 0, 32), ("ckv", 0, 128), ("iw", 0, 4), ("mi", 0, 4), ("mf", 0, 4), ("ng", 0, 12),
        ("iq", 0, 256), ("nvs", 0, 64), ("nvw", 0, 64), ("ik", 0, 64), ("qn", 0, 256),
        ("nkc", 0, 64), ("nvc", 0, 64), ("nks", 0, 64), ("nkw", 0, 64), ("nq", 0, 256), ("mq", 0, 512),
        ("mk", 0, 512), ("mv", 0, 512), ("mo", 0, 512)]
LW_W2, LW_UK, LW_UV, LW_CW, LW_CB, LW_POS, LW_END = 0, 128, 384, 640, 672, 680, 712

UNITS = [("A", 0), ("A", 1), ("S", 0), ("S", 1), ("W", 0), ("W", 1)]
FILL = [[(8 + 2 * n, 9 + 2 * n) for n in range(6)] + [(20, 21, 22, 23)],
        [(24 + n,) for n in range(6)] + [(30, 31)]]


def plan_jobs():
    jobs = []
    for l in range(DEPTH):
        if l == 0:
            jobs += [("row", i) for i in range(8)]
        jobs += [("uT", l, 0, t, k) for t in range(2) for k in range(2)]
        jobs += [(n, l) for n in ("A1_0", "A1_1", "iq", "A2", "ik", "qn", "kv", "nq", "gT", "mqk0", "mqk1",
                                  "lgE0", "lgO0", "lgE1", "lgO1", "mqk2", "mqk3", "ropeT", "ckvT",
                                  "mv0", "mv1", "vo0", "vo1", "mo", "qabsE", "qabsO", "cmph", "cmpkv",
                                  "cSE", "cSO")]
        for n in range(len(UNITS) + 1):
            if n < len(UNITS):
                jobs += [("sc", l, n, 0), ("sc", l, n, 1)]
                jobs += [("row", i) for i in FILL[l][n]]
            if n == 0:
                jobs += [("PcT", l), ("oC", l)]
            if n >= 1:
                kind, t = UNITS[n - 1]
                jobs += [("PT", l, n - 1, k) for k in range(t + 1)]
                if kind == "A":
                    jobs.append(("ol", l, n - 1))
                jobs.append(("o", l, n - 1))
        jobs += [("Mb0", l), ("Mb1", l), ("cT", l)]
        jobs += [("sM", l, h) for h in range(HEADS)]
        jobs += [("row", i) for i in FILL[l][6]]
        jobs += [("hM", l, t, p) for t in range(2) for p in range(2)]
        jobs += [("yT", l, t, k) for t in range(2) for k in range(2)]
        jobs += [("out", l, t, h) for t in range(2) for h in range(2)]
        jobs += [("uT", l, 1, t, k) for t in range(2) for k in range(2)]
    return jobs


def plan_ring():
    ring = []
    for l in range(DEPTH):
        if l == 0:
            ring += [("mod", 0, i * SLOT, SLOT, ("row", i)) for i in range(8)]
        last = ["A1_1", "A2", "qn", "nq", "mqk1", "mqk2", "mqk3", "mv1", "vo1", "mo"]
        at = 0
        for w, j in zip(PROJ, last):
            ring.append(("in", l, at * KD, w * KD, (j, l)))
            at += w
        ring += [("w1", l, j * 2048, 2048, ("cmph", l)) for j in range(2)]
        for rows in FILL[l]:
            ring += [("mod", 0, i * SLOT, SLOT, ("row", i)) for i in rows]
        ring += [("out", l, a * D, (b - a) * D, ("out", l, 1, 1)) for a, b in ((0, 3), (3, 6), (6, 8))]
        if l == 0:
            ring += [("ffn", 0, i * SLOT, SLOT, i // 2) for i in range(2 * C_DENSE)]
    return ring


JOBS = plan_jobs()
SLOTS = plan_ring()
MOE0 = len(SLOTS)
assert MOE0 % RING == 0 and (2 * C_EXP) % RING == 0


def build_trunk(nc, dram, out):
    place = {name: (i % 8, i // 8) for i, name in enumerate(JOBS)}
    slot_of = {}
    for n, (arr, l, col, w, _) in enumerate(SLOTS):
        slot_of.setdefault((arr, l), []).append(n)

    with ExitStack() as ctx:
        def sb(name, shape, dt=F32):
            return ctx.enter_context(nc.sbuf_tensor(name, shape, dt))

        sems = {}

        def S(name):
            if name not in sems:
                sems[name] = ctx.enter_context(nc.semaphore(name))
            return sems[name]

        ring = sb("ring", [P, RING, SLOT])
        x = sb("x", [P, TILES, D])
        u = sb("u", [P, TILES, D])
        uT = sb("uT", [P, KD, T])
        modss = sb("modss", [P, 2, D])
        modg = sb("modg", [P, D])
        gn = sb("gn", [P, D])
        kvn = sb("kvn", [P, D_C])
        lw = sb("lw", [P, LW_END])
        raw = sb("raw", [P, 8 * (T + 3)])
        rawv = raw[:, :].rearrange("p (b t) -> p b t", b=8)
        lnp = raw[:, 0:2 * D].rearrange("p (a n) -> p a n", a=2)
        ident = sb("ident", [P, P])
        cm = sb("cm", [P, T])
        cmT = sb("cmT", [P, T])
        cmpa = sb("cmpa", [P, TILES, N_CMP])
        cmpm = sb("cmpm", [P, TILES, N_CMP])
        ccol = sb("ccol", [P, KD])
        csil = sb("csil", [P, KD])
        bmod = sb("bmod", [32, MODW])
        rowst = sb("rowst", [1, 2, MODW])
        pos = sb("pos", [P, TILES], I32)
        ang = sb("ang", [P, TILES, 16])
        ang2 = sb("ang2", [P, TILES, 16])
        sn = sb("sn", [P, TILES, 16])
        cs = sb("cs", [P, TILES, 16])
        freq = sb("freq", [P, 16])
        A1 = sb("A1", [P, TILES, 312])
        A2 = sb("A2", [P, TILES, P])
        rot = sb("rot", [P, TILES, 8, DH_R])
        rtmp = sb("rtmp", [P, TILES, 5, 16])
        ropeT = sb("ropeT", [P, 3, T])
        ones, before = ropeT[:, 0, 0:P], ropeT[:, 1, 0:P]
        ckvn = sb("ckvn", [P, TILES, D_C])
        ckvT = sb("ckvT", [P, T])
        ik2 = sb("ik2", [P, T])
        kc2 = sb("kc2", [P, 2, T])
        ks2 = sb("ks2", [P, T])
        kw2 = sb("kw2", [P, T])
        blk = sb("blk", [P, 2, 16, N_CMP])
        r3 = sb("r3", [P, 2560])
        iqT = r3[:, 0:512].rearrange("p (b t) -> p b t", b=2)
        qnT = r3[:, 512:1024].rearrange("p (b t) -> p b t", b=2)
        nqT = r3[:, 1024:1536].rearrange("p (b t) -> p b t", b=2)
        qabsT = r3[:, 1536:2560].rearrange("p (h t) -> p h t", h=4)
        gwT = r3[:, 0:512].rearrange("p (j t) -> p j t", j=2)
        hbuf = r3[:, 512:1024].rearrange("p (j f) -> p j f", j=2)
        sgb = r3[:, 1024:1536].rearrange("p (j f) -> p j f", j=2)
        hT = r3[:, 1536:2048].rearrange("p (j b s) -> p j b s", j=2, b=2)
        prob = sb("prob", [P, 2, HEADS, T])
        yacc = prob[:, :, :, :].rearrange("p a h t -> p a (h t)")
        r2 = sb("r2", [P, 3072])
        PTs = r2[:, 0:1024].rearrange("p (k n) -> p k n", k=2)
        rel = r2[:, 0:1024].rearrange("p (h t) -> p h t", h=4)
        olT = r2[:, 1024:1536].rearrange("p (h t) -> p h t", h=4)
        Dm = r2[:, 1536:3072].rearrange("p (h t) -> p h t", h=4)
        oe = r2[:, 0:2048].rearrange("p (j n) -> p j n", j=2)
        gsel = r2[:, 2048:2560].rearrange("p (t s) -> p t s", t=2)
        gwsel = r2[:, 2560:3072].rearrange("p (t s) -> p t s", t=2)
        score = sb("score", [P, TILES, T])
        iota, iotai = score[:, 0, :], score[:, 1, :].bitcast(I32)
        mvt = sb("mvt", [P, TILES, HEADS, DH_B + 1])
        mog = sb("mog", [P, TILES, 512])
        ct = sb("ct", [P, 2, T])
        rows = modss[0:HEADS, :, :].rearrange("p a n -> p (a n)")
        gi, gf, lse, crow, brow = (rows[:, i * T:(i + 1) * T] for i in range(5))
        scanA, scanB = (rows[:, 5 * T + i * (P + T):5 * T + (i + 1) * (P + T)] for i in range(2))
        gbt = sb("gbt", [HEADS, 2])
        ccl = sb("ccl", [P, 8])
        emc = sb("emc", [P, 8])
        hid = sb("hid", [P, 2, N_CMP])
        kcmp = sb("kcmp", [P, N_CMP])
        vbd = sb("vbd", [P, HEADS, DH_C])
        Pc = sb("Pc", [P, TILES, HEADS, 32])
        PcT = rot[:, 0, :, :].rearrange("p h r -> p (h r)")
        gates = sb("gates", [P, TILES, 12])
        mx = sb("mx", [P, 6, HEADS])
        rs = sb("rs", [P, 6, HEADS])
        st8 = sb("st8", [P, TILES, HEADS])
        st8b = sb("st8b", [P, TILES, HEADS])
        max8 = sb("max8", [P, 8])
        dn = sb("dn", [P, 4])
        ss = sb("ss", [P, TILES, 16])
        ssb = sb("ssb", [P, TILES, 4])
        rstd = sb("rstd", [P, TILES, 16])
        kvs = sb("kvs", [P, 4])
        bst = sb("bst", [P, TILES, 2, 6])
        mv2 = sb("mv2", [P, TILES, 2])
        lsd = sb("lsd", [P, TILES])
        eps5 = sb("eps5", [P, 1])
        eps6 = sb("eps6", [P, 1])
        router = sb("router", [P, KD, EXPERTS])
        lg = sb("lg", [P, TILES, EXPERTS])
        top8 = sb("top8", [P, TILES, EXPERTS])
        idx8 = sb("idx8", [P, TILES, EXPERTS], U32)
        idxf = sb("idxf", [P, TILES, EXPERTS])
        w12 = sb("w12", [P, TILES, 2])
        oh = sb("oh", [P, 2, TILES, EXPERTS])
        routed = sb("routed", [P, TILES, EXPERTS])
        table = sb("table", [P, 2 * TILES, EXPERTS])
        now = sb("now", [P, 2 * TILES])
        flag = sb("flag", [1, EXPERTS], I32)
        modrow = nc.dram_tensor("modrow", (2 * DEPTH, 3 * D), F32)

        ps = ctx.enter_context(nc.psum_tensor("ps", [P, 8, 512], F32))
        GU, TB, XB, ACC = 0, 2, 3, 4

        def bank(*job):
            return ps[:, place[job][0], :]

        def full(eng, *job):
            b, use = place[job]
            eng.wait_ge(S(f"bank_full{b}"), use + 1)

        def emptied(*job):
            return S(f"bank_free{place[job][0]}")

        def copied(eng, *job):
            b, use = place[job]
            eng.wait_ge(S(f"bank_free{b}"), use + 1)

        def slot_full(eng, n, more=0):
            eng.wait_ge(S(f"slot_full{n % RING}"), 16 * (n // RING + 1) + more)

        def chain(eng, name):
            count = [0]

            def link(ins):
                count[0] += 1
                ins.then_inc(S(name), 1)
                eng.wait_ge(S(name), count[0])
            return link

        for b in range(8):
            S(f"bank_full{b}")
            S(f"bank_free{b}")
        for b in range(RING):
            S(f"slot_full{b}")

        block = ctx.enter_context(nc.Block())

        @block.sync
        def _(sp):
            src = {"mod": dram["mod"], "in": dram["w_in"], "w1": dram["w1"], "out": dram["w_out"], "ffn": dram["ffn"]}
            sp.dma_start(ccol[:, :], dram["c"]).then_inc(S("c_in"), 16)

            def load(n):
                if n >= RING:
                    last = SLOTS[n - RING][4]
                    if isinstance(last, int):
                        sp.wait_ge(S("down_done"), last + 1)
                    else:
                        full(sp, *last)
                if n < MOE0:
                    arr, l, col, w, _ = SLOTS[n]
                    a = src[arr]
                    if arr in ("mod", "ffn"):
                        s = a[col // SLOT]
                    elif arr == "in":
                        s = a[l, col * P:(col + w) * P].rearrange("(p n) -> p n", p=P)
                    else:
                        s = a[l, :, col:col + w]
                    sp.dma_start(ring[:, n % RING, 0:w], s).then_inc(S(f"slot_full{n % RING}"), 16)
                else:
                    sp.dma_start(ring[:, n % RING, :], dram["moe"][n - MOE0]).then_inc(S(f"slot_full{n % RING}"), 16)

            for n in range(MOE0 + RING):
                load(n)
                if n == 1:
                    sp.dma_start(x[:, :, :], dram["x"].rearrange("(t p) n -> p t n", p=P)).then_inc(S("x_in"), 16)

            def load_expert(e, q):
                sp.wait_ge(S("down_done"), (q - RING) // 2 + 1 + C_DENSE + C_EXP * e)
                sp.dma_start(ring[:, q % RING, :],
                             dram["moe"][bass.ds(e * (2 * C_EXP) + q, 1)].rearrange("a p n -> p (a n)")
                             ).then_inc(S(f"slot_full{q % RING}"), 16)

            with sp.Fori(0, EXPERTS - 1) as e:
                for q in range(RING, 2 * C_EXP + RING):
                    load_expert(e, q)
            for q in range(RING, 2 * C_EXP):
                load_expert(EXPERTS - 1, q)
            sp.wait_ge(S("x_done"), 2 * DEPTH)
            sp.dma_start(out.rearrange("(t p) n -> p t n", p=P), x[:, :, :]).then_inc(S("stored"), 16)
            sp.wait_ge(S("stored"), 16)

        @block.gpsimd
        def _(pool):
            link = chain(pool, "pool_order")
            g = nc.gpsimd
            g.memset(ident[:, :], 0.0)
            g.memset(cm[:, :], 0.0)
            g.memset(cmT[:, :], 0.0)
            g.memset(cmpa[:, :, :], 0.0)
            g.memset(cmpm[:, :, :], 1.0)
            g.memset(vbd[:, :, :], 0.0)
            g.memset(Pc[:, :, :, :], 0.0)
            link(g.memset(mvt[:, :, :, DH_B:DH_B + 1], 1.0))
            g.affine_select(out=ident[:, :], in_=ident[:, :], compare_op=ALU.not_equal, fill=1.0, base=0,
                            pattern=[[-1, P]], channel_multiplier=1)
            g.affine_select(out=cm[:, P:T], in_=cm[:, P:T], compare_op=ALU.is_ge, fill=NEG, base=0,
                            pattern=[[-1, P]], channel_multiplier=1)
            g.affine_select(out=cmT[:, 0:P], in_=cmT[:, 0:P], compare_op=ALU.is_ge, fill=NEG, base=0,
                            pattern=[[1, P]], channel_multiplier=-1)
            for m, fill in ((cmpa, NEG), (cmpm, 0.0)):
                ins = g.affine_select(out=m[:, :, :], in_=m[:, :, :], compare_op=ALU.is_ge, fill=fill, base=-31,
                                pattern=[[P, TILES], [-16, N_CMP]], channel_multiplier=1)
            ins.then_inc(S("consts"), 1)

            g.dma_start(bmod[:, :], dram["b_mod"]).then_inc(S("bmod_in"), 16)
            g.dma_start(pos[:, :], dram["positions"]).then_inc(S("pos_in"), 16)
            g.dma_start(freq[:, :], dram["inv_freq"].partition_broadcast(P)).then_inc(S("pos_in"), 16)
            g.dma_start(router[:, :, :], dram["router"]).then_inc(S("router_in"), 16)

            def load_small(l):
                g.dma_start(lw[:, :], dram["lw"][l]).then_inc(S("small_in"), 16)
                g.dma_start(gn[:, :], dram["grp_norm"][l].partition_broadcast(P)).then_inc(S("small_in"), 16)
                g.dma_start(kvn[:, :], dram["kv_norm"][l].partition_broadcast(P)).then_inc(S("small_in"), 16)
                g.dma_start(gbt[:, :], dram["gate_b"][l]).then_inc(S("small_in"), 16)

            def store_row(i):
                copied(pool, "row", i)
                half, part = divmod(i, 8)
                g.dma_start(modrow[half:half + 1, part * MODW:(part + 1) * MODW],
                            rowst[:, i % 2, :]).then_inc(S(f"row_stored{i % 2}"), 16)

            def load_mod(half):
                for i in range(2):
                    pool.wait_ge(S(f"row_stored{i}"), 64 * (half + 1))
                if half:
                    pool.wait_ge(S("u_done"), half)
                g.dma_start(modss[:, :, :].rearrange("p a n -> p (a n)"),
                            modrow[half, 0:2 * D].partition_broadcast(P)).then_inc(S("modss_in"), 16)

            def load_gate(half):
                if half:
                    pool.wait_ge(S("z_done"), half)
                g.dma_start(modg[:, :], modrow[half, 2 * D:3 * D].partition_broadcast(P)
                            ).then_inc(S("modg_in"), 16)

            def load_ln(half):
                g.dma_start(lnp, dram["ln"][half].partition_broadcast(P)).then_inc(S("ln_in"), 16)

            def rope(l):
                copied(pool, "A1_1", l)
                if l == 0:
                    pool.wait_ge(S("angles"), 1)
                if l > 0:
                    full(pool, "ropeT", l - 1)
                v = A1[:, :, 0:160].rearrange("p t (h r) -> p t h r", h=5)
                c5 = cs[:, :, :].unsqueeze(2).broadcast_to([P, TILES, 5, 16])
                s5 = sn[:, :, :].unsqueeze(2).broadcast_to([P, TILES, 5, 16])
                o1, o2 = rot[:, :, 0:5, 0:16], rot[:, :, 0:5, 16:32]
                g.tensor_tensor(o1, v[:, :, :, 0:16], c5, ALU.mult)
                link(g.tensor_tensor(rtmp[:, :, :, :], v[:, :, :, 16:32], s5, ALU.mult))
                g.tensor_tensor(o1, o1, rtmp[:, :, :, :], ALU.subtract)
                link(g.tensor_tensor(o2, v[:, :, :, 0:16], s5, ALU.mult))
                link(g.tensor_tensor(rtmp[:, :, :, :], v[:, :, :, 16:32], c5, ALU.mult))
                link(g.tensor_tensor(o2, o2, rtmp[:, :, :, :], ALU.add))
                for t in range(TILES):
                    last = g.tensor_copy(rot[:, t, 5:8, :], rot[:, t, 4:5, :].broadcast_to([P, 3, DH_R]))
                last.then_inc(S("rope_done"), 1)

            def gate_scans(l):
                pool.wait_ge(S("lse_done"), l + 1)
                g.memset(scanA[:, 0:P], 0.0)
                g.memset(scanB[:, 0:P], 0.0)
                a, b = scanA[:, P:P + T], scanB[:, P:P + T]
                link(g.tensor_scalar(brow[:, :], gf[:, :], 0.0, None, ALU.min))
                link(g.tensor_tensor(a, brow[:, :], lse[:, :], ALU.subtract))

                src, dst = scanA, scanB
                for d in SHIFTS:
                    link(g.tensor_tensor(dst[:, P:P + T], src[:, P:P + T], src[:, P - d:P + T - d], ALU.add))
                    src, dst = dst, src
                g.tensor_copy(brow[:, :], a)
                link(g.tensor_tensor(crow[:, :], gi[:, :], a, ALU.subtract))
                g.tensor_copy(b, crow[:, :]).then_inc(S("sums_done"), 1)

            load_small(0)
            for l in range(DEPTH):
                if l == 0:
                    for i in range(8):
                        store_row(i)
                load_mod(2 * l)
                load_gate(2 * l)
                if l:
                    pool.wait_ge(S("x_done"), 2 * l)
                g.memset(rawv[:, :, 0:3], 0.0).then_inc(S("raw_padded"), 1)
                rope(l)
                gate_scans(l)
                for rows in FILL[l]:
                    for i in rows:
                        store_row(i)
                full(pool, "cT", l)
                load_mod(2 * l + 1)
                full(pool, "sM", l, 3)
                load_ln(2 * l)
                load_gate(2 * l + 1)
                pool.wait_ge(S("x_done"), 2 * l + 1)
                load_ln(2 * l + 1)
                if l + 1 < DEPTH:
                    load_small(l + 1)
            link(g.iota(iotai, pattern=[[1, T]], base=0, channel_multiplier=0))
            link(g.tensor_copy(iota, iotai))
            g.memset(ones, 1.0)
            link(g.memset(before, 1.0))
            g.affine_select(out=before, in_=before, compare_op=ALU.is_gt, fill=0.0, base=0,
                            pattern=[[1, P]], channel_multiplier=-1).then_inc(S("iota_ready"), 1)

        @block.tensor
        def _(pe):
            order = iter(JOBS)
            mm = nc.tensor.matmul
            tr = nc.tensor.transpose

            def begin(*job):
                assert next(order) == job, job
                b, use = place[job]
                if use:
                    pe.wait_ge(S(f"bank_free{b}"), use)
                return ps[:, b, :]

            def end(ins, *job):
                ins.then_inc(S(f"bank_full{place[job][0]}"), 1)

            waited = set()

            def weights(arr, l, i):
                n = slot_of[arr, l][i]
                if n not in waited:
                    slot_full(pe, n)
                    waited.add(n)
                return ring[:, n % RING, :]

            def row(i):
                o = begin("row", i)
                w = weights("mod", 0, i).rearrange("p (k n) -> p k n", k=KD)
                for k in range(KD):
                    mm(o[0:1, 0:MODW], csil[:, k:k + 1], w[:, k, :], start=(k == 0), stop=False)
                end(mm(o[0:1, 0:MODW], ident[0:32, i:i + 1], bmod[:, :], start=False, stop=True), "row", i)

            def transposes(src, name, l, *tag):
                for t in range(TILES):
                    for kk in range(2):
                        o = begin(name, l, *tag, t, kk)
                        for i in range(4):
                            k = 4 * kk + i
                            ins = tr(o[:, i * P:(i + 1) * P], src[:, t, k * P:(k + 1) * P], ident[:, :])
                        end(ins, name, l, *tag, t, kk)

            def proj_rows(o, w, a, b, t):
                for k in range(KD):
                    ins = mm(o, uT[:, k, t * P:(t + 1) * P], w[:, k, a:b], start=(k == 0), stop=(k == KD - 1))
                return ins

            def proj_cols(o, w, a, b):
                for k in range(KD):
                    ins = mm(o, w[:, k, a:b], uT[:, k, :], start=(k == 0), stop=(k == KD - 1))
                return ins

            def mixer(l):
                if l == 0:
                    pe.wait_ge(S("consts"), 1)
                    pe.wait_ge(S("bmod_in"), 16)
                    pe.wait_ge(S("csil_done"), 1)
                    for i in range(8):
                        row(i)
                pe.wait_ge(S("u_done"), 2 * l + 1)
                transposes(u, "uT", l, 0)

                def win(i):
                    return weights("in", l, i)[:, 0:KD * PROJ[i]].rearrange("p (k n) -> p k n", k=KD)

                copied(pe, "uT", l, 0, 1, 1)
                w = win(0)
                for t in range(2):
                    o = begin(f"A1_{t}", l)
                    end(proj_rows(o[:, 0:312], w, 0, 312, t), f"A1_{t}", l)
                w = win(1)
                o = begin("iq", l)
                for b in range(2):
                    ins = proj_cols(o[:, b * T:(b + 1) * T], w, b * P, (b + 1) * P)
                end(ins, "iq", l)
                o = begin("A2", l)
                for t in range(2):
                    ins = proj_rows(o[:, t * P:(t + 1) * P], w, 256, 384, t)
                end(ins, "A2", l)
                w = win(2)
                o = begin("ik", l)
                end(proj_cols(o[0:64, 0:T], w, 0, 64), "ik", l)
                o = begin("qn", l)
                for b in range(2):
                    ins = proj_cols(o[:, b * T:(b + 1) * T], w, 64 + b * P, 64 + (b + 1) * P)
                end(ins, "qn", l)
                w = win(3)
                o = begin("kv", l)
                for b in range(2):
                    ins = proj_cols(o[:, b * T:(b + 1) * T], w, b * P, (b + 1) * P)
                end(ins, "kv", l)
                o = begin("nq", l)
                proj_cols(o[:, 0:T], w, 256, 384)
                w = win(4)
                end(proj_cols(o[:, T:2 * T], w, 0, P), "nq", l)
                o = begin("gT", l)
                copied(pe, "A1_1", l)
                for a in range(2):
                    for t in range(2):
                        ins = tr(o[0:4, (2 * a + t) * P:(2 * a + t + 1) * P], A1[:, t, 292 + 4 * a:296 + 4 * a],
                                 ident[:, :])
                end(ins, "gT", l)

                def mqk(i):
                    o = begin(f"mqk{i}", l)
                    for j in range(2):
                        b = 2 * i + j + 1
                        ins = proj_cols(o[:, j * T:(j + 1) * T], win(4 + b // 3), (b % 3) * P, (b % 3 + 1) * P)
                    end(ins, f"mqk{i}", l)
                mqk(0)
                mqk(1)
                copied(pe, "iq", l)
                copied(pe, "ik", l)
                for t in range(2):
                    for odd, name in enumerate(("lgE", "lgO")):
                        o = begin(f"{name}{t}", l)
                        n = (t + 1) * P
                        for i in range(2):
                            r = slice(64 * odd, 64 * odd + 64)
                            ins = mm(o[:, i * T:i * T + n], iqT[r, i, t * P:(t + 1) * P], ik2[r, 0:n],
                                     start=True, stop=True)
                        end(ins, f"{name}{t}", l)
                mqk(2)
                mqk(3)
                o = begin("ropeT", l)
                pe.wait_ge(S("rope_done"), l + 1)
                for a in range(2):
                    for t in range(2):
                        ins = tr(o[:, (2 * a + t) * P:(2 * a + t + 1) * P],
                                 rot[:, t, 4 * a:4 * a + 4, :].rearrange("p h r -> p (h r)"), ident[:, :])
                end(ins, "ropeT", l)
                o = begin("ckvT", l)
                pe.wait_ge(S("ckvn_done"), l + 1)
                for t in range(2):
                    ins = tr(o[:, t * P:(t + 1) * P], ckvn[:, t, :], ident[:, :])
                end(ins, "ckvT", l)
                w = win(7)
                for t in range(2):
                    o = begin(f"mv{t}", l)
                    end(proj_rows(o[:, 0:384], w, 0, 384, t), f"mv{t}", l)
                w = win(8)
                for t in range(2):
                    o = begin(f"vo{t}", l)
                    end(proj_rows(o[:, 0:384], w, 0, 384, t), f"vo{t}", l)
                w = win(9)
                o = begin("mo", l)
                for t in range(2):
                    ins = proj_rows(o[:, t * 256:(t + 1) * 256], w, 0, 256, t)
                end(ins, "mo", l)
                copied(pe, "qn", l)
                pe.wait_ge(S("small_in"), 64 * (l + 1))
                for odd, name in enumerate(("qabsE", "qabsO")):
                    o = begin(name, l)
                    for i in range(2):
                        r = slice(64 * odd, 64 * odd + 64)
                        ins = mm(o[:, i * T:(i + 1) * T], lw[r, LW_UK + i * P:LW_UK + (i + 1) * P], qnT[r, i, :],
                                 start=True, stop=True)
                    end(ins, name, l)
                o = begin("cmph", l)
                pe.wait_ge(S("blk_done"), l + 1)
                for j in range(2):
                    w = weights("w1", l, j)
                    for c in range(16):
                        ins = mm(o[:, j * N_CMP:(j + 1) * N_CMP], w[:, c * P:(c + 1) * P], blk[:, j, c, :],
                                 start=(c == 0), stop=(c == 15))
                end(ins, "cmph", l)
                o = begin("cmpkv", l)
                copied(pe, "cmph", l)
                mm(o[0:64, 0:N_CMP], lw[:, LW_W2:LW_W2 + 64], hid[:, 0, :], start=True, stop=True)
                end(mm(o[0:N_CMP, 64:128], hid[:, 1, :], lw[:, LW_W2 + 64:LW_W2 + 128], start=True, stop=True),
                    "cmpkv", l)
                copied(pe, "nq", l)
                copied(pe, "cmpkv", l)
                for odd, name in enumerate(("cSE", "cSO")):
                    o = begin(name, l)
                    r = slice(64 * odd, 64 * odd + 64)
                    for t in range(2):
                        for i in range(2):
                            c = (2 * t + i) * N_CMP
                            ins = mm(o[:, c:c + N_CMP], nqT[r, i, t * P:(t + 1) * P], kcmp[r, :],
                                     start=True, stop=True)
                    end(ins, name, l)

                def scores(n):
                    kind, t = UNITS[n]
                    m = (t + 1) * P
                    if kind == "A" and t == 0:
                        copied(pe, "qabsO", l)
                        copied(pe, "ropeT", l)
                        copied(pe, "ckvT", l)
                    if n == 2:
                        copied(pe, "kv", l)
                        copied(pe, "A2", l)
                    for part in range(2):
                        o = begin("sc", l, n, part)
                        for i in range(2):
                            if kind == "A":
                                h = part + 2 * i
                                mm(o[:, i * T:i * T + m], qabsT[:, h, t * P:(t + 1) * P], ckvT[:, 0:m],
                                   start=True, stop=False)
                                r = slice(64 * part, 64 * part + 32)
                                ins = mm(o[:, i * T:i * T + m], ropeT[r, i, t * P:(t + 1) * P], ropeT[r, 2, 0:m],
                                         start=False, stop=True)
                            else:
                                r = slice(64 * part, 64 * part + 64)
                                keys = ks2 if kind == "S" else kw2
                                ins = mm(o[:, i * T:i * T + m], nqT[r, i, t * P:(t + 1) * P], keys[r, 0:m],
                                         start=True, stop=True)
                        end(ins, "sc", l, n, part)

                def attend(n):
                    kind, t = UNITS[n]
                    pe.wait_ge(S("exp_done"), 6 * l + n + 1)
                    for kb in range(t + 1):
                        o = begin("PT", l, n, kb)
                        for h in range(HEADS):
                            ins = tr(o[:, h * P:(h + 1) * P], prob[:, n % 2, h, kb * P:(kb + 1) * P], ident[:, :])
                        end(ins, "PT", l, n, kb)
                    if kind == "A":
                        o = begin("ol", l, n)
                        copied(pe, "PT", l, n, t)
                        for kb in range(t + 1):
                            ins = mm(o[:, :], ckvn[:, kb, :], PTs[:, kb, :], start=(kb == 0), stop=(kb == t))
                        end(ins, "ol", l, n)
                        o = begin("o", l, n)
                        copied(pe, "ol", l, n)
                        for h in range(HEADS):
                            hh = ORDER[h]
                            ins = mm(o[:, h * 64:(h + 1) * 64], olT[:, h, :],
                                     lw[:, LW_UV + hh * 64:LW_UV + (hh + 1) * 64], start=True, stop=True)
                        end(ins, "o", l, n)
                    else:
                        o = begin("o", l, n)
                        copied(pe, "PT", l, n, t)
                        c = 0 if kind == "S" else 64
                        for h in range(HEADS):
                            hh = ORDER[h]
                            for kb in range(t + 1):
                                ins = mm(o[:, hh * 64:(hh + 1) * 64], PTs[:, kb, h * P:(h + 1) * P],
                                         A2[:, kb, c:c + 64], start=(kb == 0), stop=(kb == t))
                        end(ins, "o", l, n)

                for n in range(len(UNITS) + 1):
                    if n < len(UNITS):
                        scores(n)
                        for i in FILL[l][n]:
                            row(i)
                    if n == 0:
                        o = begin("PcT", l)
                        pe.wait_ge(S("Pc_done"), l + 1)
                        for t in range(2):
                            ins = tr(o[:, t * P:(t + 1) * P], Pc[:, t, :, :].rearrange("p h n -> p (h n)"), ident[:, :])
                        end(ins, "PcT", l)
                        o = begin("oC", l)
                        copied(pe, "PcT", l)
                        for t in range(2):
                            ins = mm(o[:, t * 256:(t + 1) * 256], PcT[:, t * P:(t + 1) * P],
                                     vbd[:, :, :].rearrange("p h d -> p (h d)"), start=True, stop=True)
                        end(ins, "oC", l)
                    if n >= 1:
                        attend(n - 1)

                pe.wait_ge(S("scans_done"), l + 1)
                for p in range(2):
                    o = begin(f"Mb{p}", l)
                    for i in range(2):
                        ins = mm(o[:, i * T:(i + 1) * T], ident[0:HEADS, 2 * p + i:2 * p + i + 1].broadcast_to([HEADS, P]),
                                 scanB[:, P:P + T], start=True, stop=True)
                    end(ins, f"Mb{p}", l)
                o = begin("cT", l)
                for a, r in enumerate((crow, brow)):
                    for t in range(2):
                        c = 8 * a + 4 * t
                        ins = tr(o[:, c:c + 4], r[:, t * P:(t + 1) * P], ident[0:4, 0:4])
                end(ins, "cT", l)
                pe.wait_ge(S("conv_done"), 8 * (l + 1))
                for h in range(HEADS):
                    o = begin("sM", l, h)
                    q, k = rawv[:, h, 3:3 + T], rawv[:, 4 + h, 3:3 + T]
                    mm(o[:, 0:T], k[:, 0:P], q, start=True, stop=True)
                    end(mm(o[:, T:T + P], k[:, P:T], q[:, P:T], start=True, stop=True), "sM", l, h)
                for i in FILL[l][6]:
                    row(i)
                copied(pe, "vo1", l)
                for t in range(2):
                    for p in range(2):
                        o = begin("hM", l, t, p)
                        copied(pe, "sM", l, 2 * p + 1)
                        for i in range(2):
                            h = 2 * p + i
                            for kb in range(t + 1):
                                a = t * P if kb == 0 else T
                                ins = mm(o[:, i * 129:(i + 1) * 129], Dm[:, h, a:a + P], mvt[:, kb, h, :],
                                         start=(kb == 0), stop=(kb == t))
                        end(ins, "hM", l, t, p)

                pe.wait_ge(S("y_done"), l + 1)
                transposes(u, "yT", l)
                copied(pe, "yT", l, 1, 1)
                for t in range(2):
                    for half in range(2):
                        o = begin("out", l, t, half)
                        for k in range(KD):
                            w = weights("out", l, k // 3)
                            c = (k % 3) * D + half * 512
                            ins = mm(o[:, :], uT[:, k, t * P:(t + 1) * P], w[:, c:c + 512],
                                     start=(k == 0), stop=(k == KD - 1))
                        end(ins, "out", l, t, half)
                pe.wait_ge(S("u_done"), 2 * l + 2)
                transposes(u, "uT", l, 1)
                last_use = {}
                for job in JOBS[:JOBS.index(("uT", l, 1, 1, 1)) + 1]:
                    last_use[place[job][0]] = job
                for job in last_use.values():
                    copied(pe, *job)

            def swiglu(nb, chunks, first, slots):
                n0, more = slots
                for c in range(chunks + 1):
                    if c > 0:
                        pe.wait_ge(S("h_ready"), first + c)
                        for j in range(nb):
                            for b in range(2):
                                ins = tr(ps[:, TB, (2 * j + b) * P:(2 * j + b + 1) * P],
                                         hbuf[:, j, b * P:(b + 1) * P], ident[:, :])
                        ins.then_inc(S("hT_filled"), 1)
                    if c < chunks:
                        for s in range(2):
                            slot_full(pe, n0 + 2 * c + s, more)
                        for j in range(nb):
                            for k in range(KD):
                                w = ring[:, (n0 + 2 * c + k // 4) % RING, (k % 4) * 512:(k % 4 + 1) * 512]
                                ins = mm(ps[:, GU + j, :], uT[:, k, j * P:(j + 1) * P], w,
                                         start=(k == 0), stop=(k == KD - 1))
                        ins.then_inc(S("gu_filled"), 1)
                    if c > 0:
                        pe.wait_ge(S("hT_ready"), first + c)
                        for j in range(nb):
                            for b in range(2):
                                w = ring[:, (n0 + 2 * (c - 1) + b) % RING, 2048:3072]
                                for half in range(2):
                                    ins = mm(ps[:, ACC + 2 * j + half, :], hT[:, j, b, :],
                                             w[:, half * 512:(half + 1) * 512],
                                             start=(c == 1 and b == 0), stop=(c == chunks and b == 1))
                        ins.then_inc(S("down_done"), 1)

            def expert(e, nb):
                pe.wait_ge(S("sel_ready"), e + 1)
                for kp in range(4):
                    for i in range(2):
                        k = 2 * kp + i
                        for t in range(TILES):
                            ins = mm(ps[:, kp, i * T:i * T + nb * P], u[:, t, k * P:(k + 1) * P],
                                     gsel[:, t, 0:nb * P], start=(t == 0), stop=(t == 1))
                    ins.then_inc(S("gather_filled"), 1)
                pe.wait_ge(S("gather_ready"), 4 * e + 4)
                for j in range(nb):
                    for t in range(TILES):
                        ins = tr(ps[:, XB, j * T + t * P:j * T + (t + 1) * P], gwsel[:, t, j * P:(j + 1) * P],
                                 ident[:, :])
                ins.then_inc(S("gwT_filled"), 1)
                swiglu(nb, C_EXP, C_EXP * e + C_DENSE, (MOE0, 16 * (2 * C_EXP // RING) * e))
                pe.wait_ge(S("gwT_ready"), e + 1)
                pe.wait_ge(S("oe_ready"), e + 1)
                for t in range(TILES):
                    for half in range(2):
                        for j in range(nb):
                            ins = mm(ps[:, 2 * t + half, :], gwT[:, j, t * P:(t + 1) * P],
                                     oe[:, j, half * 512:(half + 1) * 512], start=(j == 0), stop=(j == nb - 1))
                        ins.then_inc(S("scatter_filled"), 1)
                pe.wait_ge(S("y_added"), 4 * e + 5)

            mixer(0)
            swiglu(2, C_DENSE, 0, (slot_of["ffn", 0][0], 0))
            mixer(1)
            pe.wait_ge(S("router_in"), 16)
            for t in range(TILES):
                for k in range(KD):
                    ins = mm(ps[:, XB, t * 8:(t + 1) * 8], uT[:, k, t * P:(t + 1) * P], router[:, k, :],
                             start=(k == 0), stop=(k == KD - 1))
            ins.then_inc(S("logits_filled"), 1)
            pe.wait_ge(S("routed_done"), 1)
            mm(ps[:, TB, 0:8], before[:, :], routed[:, 0, :], start=True, stop=True)
            mm(ps[:, TB, 8:16], ones[:, :], routed[:, 0, :], start=True, stop=False)
            mm(ps[:, TB, 8:16], before[:, :], routed[:, 1, :], start=False, stop=True)
            mm(ps[:, TB, 16:24], ones[:, :], routed[:, 0, :], start=True, stop=False)
            mm(ps[:, TB, 16:24], ones[:, :], routed[:, 1, :], start=False, stop=True).then_inc(S("slots_filled"), 1)
            pe.wait_ge(S("flag_ready"), 1)
            with pe.Fori(0, EXPERTS) as e:
                two = pe.value_load(flag[0:1, bass.ds(e, 1)], min_val=0, max_val=1)
                with pe.If(two > 0):
                    expert(e, 2)
                with pe.Else():
                    expert(e, 1)

        @block.scalar
        def _(act):
            link = chain(act, "act_order")
            a_ = nc.scalar.activation

            def copy(o, i):
                return a_(o, i, ACT.Copy)

            def row(i):
                full(act, "row", i)
                if i >= 2:
                    act.wait_ge(S(f"row_stored{i % 2}"), 16 * (i // 2))
                b = bank("row", i)
                copy(rowst[:, i % 2, :], b[0:1, 0:MODW]).then_inc(emptied("row", i), 1)

            def transposed(name, l, *tag):
                for t in range(TILES):
                    for kk in range(2):
                        job = (name, l, *tag, t, kk)
                        full(act, *job)
                        copy(uT[:, 4 * kk:4 * kk + 4, t * P:(t + 1) * P],
                             bank(*job).rearrange("p (k n) -> p k n", k=4)).then_inc(emptied(*job), 1)

            def mixer(l):
                if l == 0:
                    act.wait_ge(S("c_in"), 16)
                    a_(csil[:, :], ccol[:, :], ACT.Silu).then_inc(S("csil_done"), 1)
                    act.wait_ge(S("angle_folded"), 1)
                    a_(sn[:, :, :], ang[:, :, :], ACT.Sin)
                    a_(cs[:, :, :], ang2[:, :, :], ACT.Sin).then_inc(S("angles"), 1)
                    for i in range(8):
                        row(i)
                transposed("uT", l, 0)
                for t in range(2):
                    job = (f"A1_{t}", l)
                    full(act, *job)
                    copy(A1[:, t, :], bank(*job)[:, 0:312]).then_inc(emptied(*job), 1)
                job = ("iq", l)
                full(act, *job)
                copy(iqT, bank(*job).rearrange("p (b t) -> p b t", b=2)).then_inc(emptied(*job), 1)
                job = ("A2", l)
                full(act, *job)
                copy(A2[:, :, :], bank(*job)[:, 0:256].rearrange("p (b t) -> p b t", b=2)).then_inc(emptied(*job), 1)
                job = ("ik", l)
                full(act, *job)
                copy(ik2[0:64, :], bank(*job)[0:64, 0:T])
                copy(ik2[64:128, :], bank(*job)[0:64, 0:T]).then_inc(emptied(*job), 1)
                job = ("qn", l)
                full(act, *job)
                copy(qnT, bank(*job).rearrange("p (b t) -> p b t", b=2)).then_inc(emptied(*job), 1)
                job = ("nq", l)
                full(act, *job)
                copy(nqT, bank(*job).rearrange("p (b t) -> p b t", b=2)).then_inc(emptied(*job), 1)
                act.wait_ge(S("kvss"), l + 1)
                a_(kvs[:, 2:4], kvs[:, 0:2], ACT.Sqrt, scale=1.0 / D_C, bias=eps6[:, :]).then_inc(S("kvrms"), 1)
                job = ("gT", l)
                full(act, *job)
                act.wait_ge(S("small_in"), 64 * (l + 1))
                b = bank(*job)
                a_(gi[:, :], b[0:4, 0:T], ACT.Identity, bias=gbt[:, 0:1])
                a_(gf[:, :], b[0:4, T:2 * T], ACT.Identity, bias=gbt[:, 1:2]).then_inc(emptied(*job), 1)
                copied(act, *job)
                link(a_(lse[:, :], gf[:, :], ACT.Abs))
                link(a_(lse[:, :], lse[:, :], ACT.Exp, scale=-1.0))
                a_(lse[:, :], lse[:, :], ACT.Ln, bias=1.0).then_inc(S("lse_done"), 1)

                def mqk(i):
                    job = (f"mqk{i}", l)
                    full(act, *job)
                    if i == 0:
                        act.wait_ge(S("raw_padded"), l + 1)
                    copy(rawv[:, 2 * i:2 * i + 2, 3:3 + T], bank(*job).rearrange("p (b t) -> p b t", b=2)
                         ).then_inc(emptied(*job), 1)

                def relus(t):
                    for odd, name in enumerate(("lgE", "lgO")):
                        job = (f"{name}{t}", l)
                        full(act, *job)
                        if odd == 0 and t == 1:
                            act.wait_ge(S("rel_used"), 2 * l + 1)
                        n = (t + 1) * P
                        a_(rel[:, odd:odd + 3:2, 0:n], bank(*job).rearrange("p (b t) -> p b t", b=2)[:, :, 0:n],
                           ACT.Relu).then_inc(emptied(*job), 1)
                mqk(0)
                mqk(1)
                relus(0)
                relus(1)
                mqk(2)
                mqk(3)
                job = ("ropeT", l)
                full(act, *job)
                b = bank(*job)
                for h in range(HEADS):
                    copy(ropeT[64 * (h % 2):64 * (h % 2) + 32, h // 2, :], b[32 * h:32 * h + 32, 0:T])
                copy(ropeT[0:32, 2, :], b[0:32, T:2 * T])
                copy(ropeT[64:96, 2, :], b[64:96, T:2 * T]).then_inc(emptied(*job), 1)
                job = ("ckvT", l)
                full(act, *job)
                copy(ckvT[:, :], bank(*job)[:, 0:T]).then_inc(emptied(*job), 1)
                for t in range(2):
                    job = (f"mv{t}", l)
                    full(act, *job)
                    copy(mvt[:, t, 0:3, 0:DH_B], bank(*job)[:, 0:384].rearrange("p (h d) -> p h d", h=3)
                         ).then_inc(emptied(*job), 1)
                for t in range(2):
                    job = (f"vo{t}", l)
                    full(act, *job)
                    copy(mvt[:, t, 3, 0:DH_B], bank(*job)[:, 0:P])
                    a_(mog[:, t, 0:256], bank(*job)[:, P:384], ACT.Sigmoid).then_inc(emptied(*job), 1)
                job = ("mo", l)
                full(act, *job)
                a_(mog[:, :, 256:512], bank(*job).rearrange("p (t n) -> p t n", t=2), ACT.Sigmoid
                   ).then_inc(emptied(*job), 1)
                a_(gates[:, :, :], A1[:, :, 300:312], ACT.Sigmoid).then_inc(S("gates_ready"), 1)
                for odd, name in enumerate(("qabsE", "qabsO")):
                    job = (name, l)
                    full(act, *job)
                    copy(qabsT[:, odd:odd + 3:2, :], bank(*job).rearrange("p (b t) -> p b t", b=2)
                         ).then_inc(emptied(*job), 1)
                job = ("cmph", l)
                full(act, *job)
                a_(hid[:, :, :], bank(*job)[:, 0:2 * N_CMP].rearrange("p (j n) -> p j n", j=2), ACT.Silu
                   ).then_inc(emptied(*job), 1)
                job = ("cmpkv", l)
                full(act, *job)
                b = bank(*job)
                copy(kcmp[0:64, :], b[0:64, 0:N_CMP])
                copy(kcmp[64:128, :], b[0:64, 0:N_CMP])
                for h in range(HEADS):
                    ins = copy(vbd[32 * h:32 * h + N_CMP, h, :], b[0:N_CMP, 64:128])
                ins.then_inc(emptied(*job), 1)
                for b in range(8):
                    act.wait_ge(S("conv_sum"), 8 * l + b + 1)
                    a_(rawv[:, b, 3:3 + T], ct[:, b % 2, :], ACT.Silu).then_inc(S("conv_done"), 1)
                act.wait_ge(S("Pc_shifted"), l + 1)
                a_(Pc[:, :, :, 0:N_CMP], Pc[:, :, :, 0:N_CMP], ACT.Exp, scale=SCALE_C).then_inc(S("Pc_exp"), 1)

                def exps(n):
                    kind, t = UNITS[n]
                    m = (t + 1) * P
                    sc = SCALE_A if kind == "A" else SCALE_C
                    act.wait_ge(S("prob_ready"), 6 * l + n + 1)
                    for h in range(HEADS):
                        ins = a_(prob[:, n % 2, h, 0:m], prob[:, n % 2, h, 0:m], ACT.Exp, scale=sc,
                                 bias=mx[:, n, h:h + 1], accum_out=rs[:, n, h:h + 1])
                    ins.then_inc(S("exp_done"), 1)

                def turned(n):
                    kind, t = UNITS[n]
                    for kb in range(t + 1):
                        job = ("PT", l, n, kb)
                        full(act, *job)
                        if kb == 0 and n > 0:
                            full(act, "ol" if UNITS[n - 1][0] == "A" else "o", l, n - 1)
                        copy(PTs[:, kb, :], bank(*job)).then_inc(emptied(*job), 1)
                    if kind == "A":
                        job = ("ol", l, n)
                        full(act, *job)
                        copy(olT, bank(*job).rearrange("p (h t) -> p h t", h=4)).then_inc(emptied(*job), 1)

                for n in range(len(UNITS) + 1):
                    if n < len(UNITS):
                        for i in FILL[l][n]:
                            row(i)
                    if n == 0:
                        job = ("PcT", l)
                        full(act, *job)
                        copy(PcT[:, :], bank(*job)[:, 0:T]).then_inc(emptied(*job), 1)
                    if n < len(UNITS) and n == 0:
                        exps(0)
                    if n >= 1:
                        turned(n - 1)
                        if n < len(UNITS):
                            exps(n)
                job = ("cT", l)
                full(act, *job)
                copy(ccl[:, :], bank(*job)[:, 0:8])
                a_(emc[:, :], bank(*job)[:, 8:16], ACT.Exp, scale=-1.0).then_inc(emptied(*job), 1)
                copied(act, "cT", l)
                copied(act, "Mb1", l)
                for h in range(HEADS):
                    a_(Dm[:, h, 0:T], Dm[:, h, 0:T], ACT.Exp, bias=ccl[:, h:h + 1])
                    a_(Dm[:, h, T:T + P], Dm[:, h, T:T + P], ACT.Exp, bias=ccl[:, 4 + h:5 + h]
                       ).then_inc(S("Dm_exp"), 1)
                for i in FILL[l][6]:
                    row(i)
                act.wait_ge(S("ss_ready"), l + 1)
                a_(rstd[:, :, :], ss[:, :, :], ACT.Sqrt, scale=1.0 / 64, bias=eps6[:, :]).then_inc(S("rms_ready"), 1)
                transposed("yT", l)
                ln_root(2 * l)
                transposed("uT", l, 1)

            def ln_root(i):
                act.wait_ge(S("var_ready"), i + 1)
                a_(lsd[:, :], mv2[:, :, 1], ACT.Sqrt, bias=eps5[:, :]).then_inc(S("std_ready"), 1)

            def swiglu(nb, chunks, first):
                for c in range(chunks + 1):
                    if c > 0:
                        act.wait_ge(S("hT_filled"), first + c)
                        copy(hT[:, 0:nb, :, :], ps[:, TB, 0:nb * 256].rearrange("p (j b s) -> p j b s", j=nb, b=2)
                             ).then_inc(S("hT_ready"), 1)
                    if c < chunks:
                        act.wait_ge(S("gu_filled"), first + c + 1)
                        a_(sgb[:, 0:nb, :], ps[:, GU:GU + nb, 0:FC], ACT.Silu).then_inc(S("silu_done"), 1)

            def expert(e, nb):
                for kp in range(4):
                    act.wait_ge(S("gather_filled"), 4 * e + kp + 1)
                    copy(uT[:, 2 * kp:2 * kp + 2, 0:nb * P],
                         ps[:, kp, :].rearrange("p (i s) -> p i s", i=2)[:, :, 0:nb * P]).then_inc(S("gather_ready"), 1)
                act.wait_ge(S("gwT_filled"), e + 1)
                copy(gwT[:, 0:nb, :], ps[:, XB, 0:nb * T].rearrange("p (j t) -> p j t", j=nb)).then_inc(S("gwT_ready"), 1)
                swiglu(nb, C_EXP, C_EXP * e + C_DENSE)
                act.wait_ge(S("down_done"), C_EXP * (e + 1) + C_DENSE)
                for j in range(nb):
                    for half in range(2):
                        ins = copy(oe[:, j, half * 512:(half + 1) * 512], ps[:, ACC + 2 * j + half, :])
                ins.then_inc(S("oe_ready"), 1)

            act.wait_ge(S("eps_ready"), 1)
            mixer(0)
            swiglu(2, C_DENSE, 0)
            ln_root(1)
            mixer(1)
            act.wait_ge(S("gap_ready"), 1)
            a_(w12[:, :, 1], w12[:, :, 0], ACT.Exp).then_inc(S("gap_exp"), 1)
            act.wait_ge(S("flag_ready"), 1)
            with act.Fori(0, EXPERTS) as e:
                two = act.value_load(flag[0:1, bass.ds(e, 1)], min_val=0, max_val=1)
                with act.If(two > 0):
                    expert(e, 2)
                with act.Else():
                    expert(e, 1)
            ln_root(3)

        @block.vector
        def _(dve):
            link = chain(dve, "dve_order")
            v = nc.vector
            tt, tsc, stt = v.tensor_tensor, v.tensor_scalar, v.scalar_tensor_tensor

            v.memset(eps5[:, :], 1e-5)
            v.memset(eps6[:, :], 1e-6).then_inc(S("eps_ready"), 1)
            dve.wait_ge(S("pos_in"), 32)
            link(v.tensor_copy(lsd[:, :], pos[:, :]))
            for t in range(TILES):
                ins = tsc(ang[:, t, :], freq[:, :], lsd[:, t:t + 1], None, ALU.mult)
            link(ins)
            link(tsc(ang2[:, :, :], ang[:, :, :], 1.0 / TWO_PI, None, ALU.mult))
            link(tsc(ang2[:, :, :], ang2[:, :, :], 12582912.0, None, ALU.add))
            link(tsc(ang2[:, :, :], ang2[:, :, :], -12582912.0, None, ALU.add))
            for part in PI_PARTS:
                link(stt(ang[:, :, :], ang2[:, :, :], -part, ang[:, :, :], ALU.mult, ALU.add))
            link(tsc(ang[:, :, :], ang[:, :, :], PI_IN, -PI_IN, ALU.min, ALU.max))
            link(stt(ang2[:, :, :], ang[:, :, :], -1.0, ang[:, :, :], ALU.mult, ALU.max))
            tsc(ang2[:, :, :], ang2[:, :, :], -1.0, float(np.pi / 2), ALU.mult, ALU.add).then_inc(S("angle_folded"), 1)

            def modulate(half):
                dve.wait_ge(S("modss_in"), 16 * (half + 1))
                if half == 0:
                    dve.wait_ge(S("x_in"), 16)
                for t in range(TILES):
                    ins = stt(u[:, t, :], modss[:, 1, :], 1.0, x[:, t, :], ALU.add, ALU.mult)
                link(ins)
                for t in range(TILES):
                    ins = tt(u[:, t, :], u[:, t, :], modss[:, 0, :], ALU.add)
                ins.then_inc(S("u_done"), 1)

            def add_norm(half, parts):
                dve.wait_ge(S("modg_in"), 16 * (half + 1))
                for (t, h), (wait, y, give) in parts.items():
                    wait()
                    c = slice(h * 512, (h + 1) * 512)
                    ins = stt(u[:, t, c], modg[:, c], 1.0, y, ALU.add, ALU.mult)
                    if give is not None:
                        ins.then_inc(give, 1)
                if give is None:
                    link(ins)
                else:
                    copied(dve, "out", half // 2, 1, 1)
                for t in range(TILES):
                    ins = stt(x[:, t, :], x[:, t, :], ALPHA, u[:, t, :], ALU.mult, ALU.add)
                ins.then_inc(S("z_done"), 1)
                dve.wait_ge(S("z_done"), half + 1)
                for t in range(TILES):
                    for h in range(2):
                        ins = v.bn_stats(bst[:, t, h, :], x[:, t, h * 512:(h + 1) * 512])
                link(ins)
                for t in range(TILES):
                    ins = v.bn_aggr(mv2[:, t, :], bst[:, t, :, :])
                ins.then_inc(S("var_ready"), 1)
                dve.wait_ge(S("std_ready"), half + 1)
                link(v.reciprocal(lsd[:, :], lsd[:, :]))
                dve.wait_ge(S("ln_in"), 16 * (half + 1))
                for t in range(TILES):
                    ins = stt(x[:, t, :], x[:, t, :], mv2[:, t, 0:1], lnp[:, 0, :], ALU.subtract, ALU.mult)
                link(ins)
                for t in range(TILES):
                    ins = stt(x[:, t, :], x[:, t, :], lsd[:, t:t + 1], lnp[:, 1, :], ALU.mult, ALU.add)
                ins.then_inc(S("x_done"), 1)
                dve.wait_ge(S("x_done"), half + 1)

            def per_head(a, n, w):
                return a.unsqueeze(2).broadcast_to([P, n, w])

            def mixer(l):
                modulate(2 * l)
                copied(dve, "A1_1", l)
                dve.wait_ge(S("small_in"), 64 * (l + 1))
                for t in range(TILES):
                    c = A1[:, t, 160:288]
                    ins = stt(ckvn[:, t, :], c, 1.0, c, ALU.mult, ALU.mult, accum_out=kvs[:, t:t + 1])
                ins.then_inc(S("kvss"), 1)
                job = ("kv", l)
                full(dve, *job)
                b = bank(*job)
                for j, r in enumerate((slice(0, 64), slice(64, 128))):
                    v.tensor_copy(kc2[0:64, j, :], b[r, 0:T])
                    v.tensor_copy(kc2[64:128, j, 0:T - 1], b[r, 1:T])
                for dst, r in ((ks2, slice(0, 64)), (kw2, slice(64, 128))):
                    v.tensor_copy(dst[0:64, :], b[r, T:2 * T])
                    ins = v.tensor_copy(dst[64:128, :], b[r, T:2 * T])
                ins.then_inc(emptied(*job), 1)
                copied(dve, *job)
                for j in range(2):
                    src = kc2[:, j, :]
                    win = bass.AP(src.tensor, src.offset, [list(src.ap[0]), [2, 16], [16, N_CMP]])
                    pe_ = lw[:, LW_POS + 16 * j:LW_POS + 16 * (j + 1)].unsqueeze(2).broadcast_to([P, 16, N_CMP])
                    ins = tt(blk[:, j, :, :], win, pe_, ALU.add)
                ins.then_inc(S("blk_done"), 1)
                dve.wait_ge(S("kvrms"), l + 1)
                link(v.reciprocal(kvs[:, 2:4], kvs[:, 2:4]))
                for t in range(TILES):
                    ins = stt(ckvn[:, t, :], A1[:, t, 160:288], kvs[:, 2 + t:3 + t], kvn[:, :], ALU.mult, ALU.mult)
                ins.then_inc(S("ckvn_done"), 1)
                for t in range(TILES):
                    n = (t + 1) * P
                    s = score[:, t, 0:n]
                    copied(dve, f"lgO{t}", l)
                    for h in range(HEADS):
                        ins = stt(s, rel[:, h, 0:n], A1[:, t, 288 + h:289 + h], cm[:, T - n:T] if h == 0 else s,
                                  ALU.mult, ALU.add)
                        if h < HEADS - 1:
                            link(ins)
                    ins.then_inc(S("rel_used"), 1)
                    dve.wait_ge(S("rel_used"), 2 * l + t + 1)
                    for _ in range(K_SEL // 8):
                        link(v.max(max8[:, :], s))
                        link(v.match_replace(s, max8[:, :], s, TAKEN))
                    link(tsc(s, s, TAKEN / 2, NEG, ALU.is_gt, ALU.mult))
                    link(tt(s, s, cm[:, T - n:T], ALU.add))
                for b in range(8):
                    copied(dve, f"mqk{b // 2}", l)
                    if b >= 2 or l > 0:
                        dve.wait_ge(S("conv_done"), 8 * l + b - 1 if b >= 2 else 8 * l)
                    o = ct[:, b % 2, :]
                    cw = LW_CW + 4 * b
                    link(tsc(o, rawv[:, b, 0:T], lw[:, cw:cw + 1], lw[:, LW_CB + b:LW_CB + b + 1], ALU.mult, ALU.add))
                    for j in range(1, 4):
                        ins = stt(o, rawv[:, b, j:j + T], lw[:, cw + j:cw + j + 1], o, ALU.mult, ALU.add)
                        if j < 3:
                            link(ins)
                    ins.then_inc(S("conv_sum"), 1)
                dve.wait_ge(S("sums_done"), l + 1)
                src, dst = scanB, scanA
                for d in SHIFTS:
                    link(tt(dst[:, P:P + T], src[:, P:P + T], src[:, P - d:P + T - d], ALU.max))
                    src, dst = dst, src
                tt(brow[:, :], brow[:, :], scanB[:, P:P + T], ALU.add).then_inc(S("scans_done"), 1)
                pc = Pc[:, :, :, 0:N_CMP]
                for odd, name in enumerate(("cSE", "cSO")):
                    full(dve, name, l)
                    b = bank(name, l)[:, 0:4 * N_CMP].rearrange("p (t i n) -> p t i n", t=2, i=2)
                    ins = tt(pc[:, :, odd:odd + 3:2, :], b,
                             cmpa[:, :, :].unsqueeze(2).broadcast_to([P, TILES, 2, N_CMP]), ALU.add)
                    ins.then_inc(emptied(name, l), 1)
                    copied(dve, name, l)
                link(v.tensor_reduce(st8[:, :, :], pc, X, ALU.max))
                tt(pc, pc, st8[:, :, :].unsqueeze(3).broadcast_to([P, TILES, HEADS, N_CMP]), ALU.subtract
                   ).then_inc(S("Pc_shifted"), 1)
                dve.wait_ge(S("Pc_exp"), l + 1)
                link(tt(pc, pc, cmpm[:, :, :].unsqueeze(2).broadcast_to([P, TILES, HEADS, N_CMP]), ALU.mult))
                link(v.tensor_reduce(st8[:, :, :], pc, X, ALU.add))
                link(tsc(st8[:, :, :], st8[:, :, :], 1e-30, None, ALU.max))
                link(v.reciprocal(st8[:, :, :], st8[:, :, :]))
                tt(pc, pc, st8[:, :, :].unsqueeze(3).broadcast_to([P, TILES, HEADS, N_CMP]), ALU.mult
                   ).then_inc(S("Pc_done"), 1)
                dve.wait_ge(S("gates_ready"), l + 1)
                dve.wait_ge(S("conv_done"), 8 * (l + 1))

                def probs(n):
                    kind, t = UNITS[n]
                    m = (t + 1) * P
                    if n >= 2:
                        full(dve, "PT", l, n - 2, UNITS[n - 2][1])
                    mask = score[:, t, 0:m] if kind == "A" else cm[:, T - m:T]
                    for part in range(2):
                        job = ("sc", l, n, part)
                        full(dve, *job)
                        ins = tt(prob[:, n % 2, 2 * part:2 * part + 2, 0:m],
                                 bank(*job).rearrange("p (i t) -> p i t", i=2)[:, :, 0:m],
                                 mask.unsqueeze(1).broadcast_to([P, 2, m]), ALU.add)
                        ins.then_inc(emptied(*job), 1)
                    copied(dve, *job)
                    link(v.tensor_reduce(mx[:, n, :], prob[:, n % 2, :, 0:m], X, ALU.max))
                    tsc(mx[:, n, :], mx[:, n, :], -(SCALE_A if kind == "A" else SCALE_C), None, ALU.mult
                        ).then_inc(S("prob_ready"), 1)

                def outputs(n):
                    kind, t = UNITS[n]
                    dve.wait_ge(S("exp_done"), 6 * l + n + 1)
                    link(v.reciprocal(rs[:, n, :], rs[:, n, :]))
                    if kind != "A":
                        g = gates[:, t, 4:8] if kind == "S" else gates[:, t, 8:12]
                        for part in range(2):
                            ins = tt(mx[:, n, part:part + 3:2], rs[:, n, 2 * part:2 * part + 2], g[:, part:part + 3:2],
                                     ALU.mult)
                        link(ins)
                    job = ("o", l, n)
                    full(dve, *job)
                    o = bank(*job)[:, 0:256].rearrange("p (h d) -> p h d", h=4)
                    if kind == "A":
                        for part in range(2):
                            ins = tt(u[:, t, 0:256].rearrange("p (h d) -> p h d", h=4)[:, part:part + 3:2, :],
                                     o[:, 2 * part:2 * part + 2, :],
                                     per_head(rs[:, n, 2 * part:2 * part + 2], 2, 64), ALU.mult)
                        ins.then_inc(emptied(*job), 1)
                        copied(dve, *job)
                    else:
                        tmp = ct[:, 0, :].rearrange("p (h d) -> p h d", h=4)
                        y = u[:, t, 768:1024].rearrange("p (h d) -> p h d", h=4)
                        tt(tmp, o, per_head(mx[:, n, :], 4, 64), ALU.mult).then_inc(emptied(*job), 1)
                        copied(dve, *job)
                        link(tt(y, y, tmp, ALU.add))

                for n in range(len(UNITS) + 1):
                    if n < len(UNITS):
                        probs(n)
                    if n == 0:
                        job = ("oC", l)
                        full(dve, *job)
                        for t in range(TILES):
                            ins = tt(u[:, t, 768:1024].rearrange("p (h d) -> p h d", h=4),
                                     bank(*job)[:, t * 256:(t + 1) * 256].rearrange("p (h d) -> p h d", h=4),
                                     per_head(gates[:, t, 0:4], 4, 64), ALU.mult)
                        ins.then_inc(emptied(*job), 1)
                        copied(dve, *job)
                    if n >= 1:
                        outputs(n - 1)

                for p in range(2):
                    job = (f"Mb{p}", l)
                    full(dve, *job)
                    b = bank(*job).rearrange("p (i t) -> p i t", i=2)
                    stt(Dm[:, 2 * p:2 * p + 2, 0:T], b, -1.0, cmT[:, :].unsqueeze(1).broadcast_to([P, 2, T]),
                        ALU.mult, ALU.add)
                    ins = stt(Dm[:, 2 * p:2 * p + 2, T:T + P], b[:, :, P:T], -1.0,
                              cmT[:, 0:P].unsqueeze(1).broadcast_to([P, 2, P]), ALU.mult, ALU.add)
                    ins.then_inc(emptied(*job), 1)
                for h in range(HEADS):
                    job = ("sM", l, h)
                    full(dve, *job)
                    dve.wait_ge(S("Dm_exp"), 4 * l + h + 1)
                    stt(Dm[:, h, :], bank(*job)[:, 0:384], SCALE_B, Dm[:, h, :], ALU.mult, ALU.mult
                        ).then_inc(emptied(*job), 1)
                copied(dve, "cT", l)
                for t in range(TILES):
                    for p in range(2):
                        job = ("hM", l, t, p)
                        full(dve, *job)
                        b = bank(*job)[:, 0:258].rearrange("p (i d) -> p i d", i=2)
                        link(v.tensor_copy(dn[:, 0:2], b[:, :, 128]))
                        link(stt(dn[:, 2:4], dn[:, 0:2], -1.0, dn[:, 0:2], ALU.mult, ALU.max))
                        link(tt(dn[:, 2:4], dn[:, 2:4], emc[:, 4 * t + 2 * p:4 * t + 2 * p + 2], ALU.max))
                        link(v.reciprocal(dn[:, 2:4], dn[:, 2:4]))
                        ins = tt(u[:, t, 256 + 256 * p:512 + 256 * p].rearrange("p (i d) -> p i d", i=2), b[:, :, 0:128],
                                 per_head(dn[:, 2:4], 2, 128), ALU.mult)
                        ins.then_inc(emptied(*job), 1)
                        copied(dve, *job)

                sq = prob[:, :, :, :].rearrange("p a h t -> p a (h t)")
                link(tt(sq, u[:, :, :], u[:, :, :], ALU.mult))
                link(v.tensor_reduce(ss[:, :, :], sq.rearrange("p a (g d) -> p a g d", d=64), X, ALU.add))
                link(tt(ssb[:, :, :], ss[:, :, 4:12:2], ss[:, :, 5:12:2], ALU.add))
                tsc(ss[:, :, 4:12].rearrange("p t (h i) -> p t h i", i=2),
                    ssb[:, :, :].unsqueeze(3).broadcast_to([P, TILES, 4, 2]), 0.5, None, ALU.mult
                    ).then_inc(S("ss_ready"), 1)
                dve.wait_ge(S("rms_ready"), l + 1)
                link(v.reciprocal(rstd[:, :, :], rstd[:, :, :]))
                y = u[:, :, :].rearrange("p a (g d) -> p a g d", d=64)
                link(tt(y, y, rstd[:, :, :].unsqueeze(3).broadcast_to([P, TILES, 16, 64]), ALU.mult))
                link(tt(u[:, :, :], u[:, :, :], gn[:, :].unsqueeze(1).broadcast_to([P, TILES, D]), ALU.mult))
                tt(u[:, :, 256:768], u[:, :, 256:768], mog[:, :, :], ALU.mult).then_inc(S("y_done"), 1)

                parts = {}
                for t in range(TILES):
                    for h in range(2):
                        job = ("out", l, t, h)
                        parts[t, h] = ((lambda job=job: full(dve, *job)), bank(*job), emptied(*job))
                add_norm(2 * l, parts)
                modulate(2 * l + 1)

            def swiglu(nb, chunks, first):
                for c in range(chunks):
                    dve.wait_ge(S("silu_done"), first + c + 1)
                    tt(hbuf[:, 0:nb, :], sgb[:, 0:nb, :], ps[:, GU:GU + nb, FC:2 * FC], ALU.mult
                       ).then_inc(S("h_ready"), 1)

            def expert(e, nb):
                v.tensor_copy(now[:, :], table[:, :, bass.ds(e, 1)].rearrange("p a b -> p (a b)")
                              ).then_inc(S("now_ready"), 1)
                dve.wait_ge(S("y_added"), 4 * e + 1)
                dve.wait_ge(S("now_ready"), e + 1)
                for t in range(TILES):
                    tsc(gsel[:, t, 0:nb * P], iota[:, 0:nb * P], now[:, t:t + 1], None, ALU.is_equal)
                for t in range(TILES):
                    ins = tsc(gwsel[:, t, 0:nb * P], iota[:, 0:nb * P], now[:, t:t + 1], now[:, 2 + t:3 + t],
                              ALU.is_equal, ALU.mult)
                ins.then_inc(S("sel_ready"), 1)
                swiglu(nb, C_EXP, C_EXP * e + C_DENSE)
                for t in range(TILES):
                    for half in range(2):
                        i = 2 * t + half
                        dve.wait_ge(S("scatter_filled"), 4 * e + i + 1)
                        c = slice(half * 512, (half + 1) * 512)
                        tt(yacc[:, t, c], yacc[:, t, c], ps[:, i, :], ALU.add).then_inc(S("y_added"), 1)

            mixer(0)
            swiglu(2, C_DENSE, 0)
            parts = {}
            for t in range(TILES):
                for h in range(2):
                    parts[t, h] = ((lambda: dve.wait_ge(S("down_done"), C_DENSE)), ps[:, ACC + 2 * t + h, :], None)
            add_norm(1, parts)
            mixer(1)
            dve.wait_ge(S("logits_filled"), 1)
            link(v.tensor_copy(lg[:, :, :], ps[:, XB, 0:16].rearrange("p (t e) -> p t e", t=2)))
            for t in range(TILES):
                link(v.max(top8[:, t, :], lg[:, t, :]))
                link(v.max_index(idx8[:, t, :], top8[:, t, :], lg[:, t, :]))
            v.tensor_copy(idxf[:, :, :], idx8[:, :, :])
            tt(w12[:, :, 0], top8[:, :, 1], top8[:, :, 0], ALU.subtract).then_inc(S("gap_ready"), 1)
            dve.wait_ge(S("gap_ready"), 1)
            dve.wait_ge(S("iota_ready"), 1)
            for k in range(2):
                for t in range(TILES):
                    ins = tsc(oh[:, k, t, :], iota[:, 0:EXPERTS], idxf[:, t, k:k + 1], None, ALU.is_equal)
            link(ins)
            tt(routed[:, :, :], oh[:, 0, :, :], oh[:, 1, :, :], ALU.add).then_inc(S("routed_done"), 1)
            dve.wait_ge(S("gap_exp"), 1)
            link(tsc(w12[:, :, 0], w12[:, :, 1], 1.0, None, ALU.add))
            link(v.reciprocal(w12[:, :, 0], w12[:, :, 0]))
            link(tt(w12[:, :, 1], w12[:, :, 1], w12[:, :, 0], ALU.mult))
            for t in range(TILES):
                ins = tsc(oh[:, 0, t, :], oh[:, 0, t, :], w12[:, t, 0:1], None, ALU.mult)
            link(ins)
            for t in range(TILES):
                ins = stt(table[:, 2 + t, :], oh[:, 1, t, :], w12[:, t, 1:2], oh[:, 0, t, :], ALU.mult, ALU.add)
            link(ins)
            dve.wait_ge(S("slots_filled"), 1)
            link(stt(table[:, 0:2, :], ps[:, TB, 0:16].rearrange("p (t e) -> p t e", t=2), 1.0, routed[:, :, :],
                     ALU.add, ALU.mult))
            link(tsc(table[:, 0:2, :], table[:, 0:2, :], -1.0, None, ALU.add))
            v.memset(yacc, 0.0).then_inc(S("y_added"), 1)
            tsc(flag[:, :], ps[0:1, TB, 16:24], ONE_BLOCK, None, ALU.is_gt).then_inc(S("flag_ready"), 1)
            dve.wait_ge(S("flag_ready"), 1)
            with dve.Fori(0, EXPERTS) as e:
                two = dve.value_load(flag[0:1, bass.ds(e, 1)], min_val=0, max_val=1)
                with dve.If(two > 0):
                    expert(e, 2)
                with dve.Else():
                    expert(e, 1)
            dve.wait_ge(S("y_added"), 4 * EXPERTS + 1)
            parts = {(t, h): ((lambda: None), yacc[:, t, h * 512:(h + 1) * 512], None)
                     for t in range(TILES) for h in range(2)}
            add_norm(3, parts)


PI_1 = 6.28125
PI_2 = float(np.floor((TWO_PI - PI_1) * 2 ** 20) / 2 ** 20)
PI_PARTS = (PI_1, PI_2, TWO_PI - PI_1 - PI_2)
PI_IN = 3.1415925
ONE_BLOCK = 128.0
ORDER = (0, 2, 1, 3)
SHIFTS = [2 ** i for i in range(8)]


def pack(inputs):
    a = {k: np.asarray(v) for k, v in inputs.items()}
    L = DEPTH

    def swiglu(gate, up, down):
        n, f = gate.shape[0], gate.shape[2]
        c = f // FC
        out = np.empty((n, c, 2, P, SLOT), np.float32)
        gu = out[..., 0:2048].reshape(n, c, 2, P, 4, 2, FC)
        for j, w in enumerate((gate, up)):
            gu[:, :, :, :, :, j] = w.reshape(n, 2, 4, P, c, FC).transpose(0, 4, 1, 3, 2, 5)
        out[..., 0:2048] = gu.reshape(n, c, 2, P, 2048)
        out[..., 2048:] = down.reshape(n, c, 2, P, D)
        return out.reshape(n * c * 2, P, SLOT)

    cols = np.concatenate([OFF[n] + i + np.arange(w) for n, i, w in PICK])
    w = a["w_in"][:, :, cols].reshape(L, KD, P, -1)
    at, parts = 0, []
    for width in PROJ:
        parts.append(w[..., at:at + width].transpose(0, 2, 1, 3).reshape(L, -1))
        at += width
    w2, uk, uv = a["nsa_cmp_w2"], a["dsa_w_uk"], a["dsa_w_uv"]
    lw = [w2.transpose(0, 2, 1, 3).reshape(L, P, -1),
          uk.reshape(L, 2, 2, 64, D_C).transpose(0, 2, 3, 1, 4).reshape(L, P, -1),
          uv.transpose(0, 2, 1, 3).reshape(L, P, -1),
          a["mlstm_conv_w"].reshape(L, 4, 8, P).transpose(0, 3, 2, 1).reshape(L, P, -1),
          a["mlstm_conv_b"].reshape(L, 8, P).transpose(0, 2, 1),
          a["nsa_cmp_pos"].reshape(L, 2, 16, P).transpose(0, 3, 1, 2).reshape(L, P, -1)]
    return {
        "x": a["x"].reshape(T, D),
        "c": a["c"].reshape(KD, P).T,
        "positions": a["positions"].reshape(TILES, P).T,
        "inv_freq": np.float32(10000.0) ** (-np.arange(0, DH_R, 2, dtype=np.float32) / DH_R),
        "mod": a["w_mod"].reshape(KD, P, 32, MODW).transpose(2, 1, 0, 3).reshape(32, P, SLOT),
        "b_mod": a["b_mod"].reshape(32, MODW),
        "w_in": np.concatenate(parts, 1),
        "w1": a["nsa_cmp_w1"].reshape(L, 2, 16, P, P).transpose(0, 3, 1, 2, 4).reshape(L, P, -1),
        "lw": np.concatenate(lw, 2),
        "kv_norm": a["dsa_kv_norm"],
        "grp_norm": a["grp_norm"],
        "gate_b": a["mlstm_gate_b"].transpose(0, 2, 1),
        "ln": np.stack([a["ln_g"], a["ln_b"]], 2).reshape(2 * L, 2 * D),
        "w_out": a["w_out"].reshape(L, KD, P, D).transpose(0, 2, 1, 3).reshape(L, P, -1),
        "ffn": swiglu(a["ffn_w_gate"], a["ffn_w_up"], a["ffn_w_down"]),
        "router": a["moe_router"].reshape(KD, P, EXPERTS).transpose(1, 0, 2),
        "moe": swiglu(a["moe_w_gate"][0], a["moe_w_up"][0], a["moe_w_down"][0]),
    }


def kernel(**inputs):
    from concourse import bacc
    from concourse.bass_utils import run_bass_kernel_spmd

    nc = bacc.Bacc("TRN2", target_bir_lowering=False, num_devices=1)
    arrays, ins = {}, {}
    for name, a in pack(inputs).items():
        arrays[f"in_{name}"] = np.ascontiguousarray(a)
        ins[name] = nc.dram_tensor(f"in_{name}", a.shape, mybir.dt.from_np(a.dtype), kind="ExternalInput").ap()
    out = nc.dram_tensor("out_0", (T, D), F32, kind="ExternalOutput").ap()
    build_trunk(nc, ins, out)
    r = run_bass_kernel_spmd(nc, [arrays], core_ids=[0])
    return r.results[0]["out_0"].reshape(1, T, D)
```

```python
from contextlib import ExitStack

import numpy as np

import concourse.bass as bass
from concourse import mybir

F32 = mybir.dt.float32
I32 = mybir.dt.int32
U32 = mybir.dt.uint32
ALU = mybir.AluOpType
ACT = mybir.ActivationFunctionType
X = mybir.AxisListType.X

P = 128
D = 1024
T = 256
TILES = T // P
DEPTH = 2
KD = D // P
HEADS = 4
DH_V = 64
D_C = 128
DH_R = 32
DH_B = 128
DH_C = 64
K_SEL = T // 4
N_CMP = (T - 32) // 16 + 1
F_DENSE = 2816
F_EXP = 3584
EXPERTS = 8
ALPHA = (2 * DEPTH) ** 0.25
SCALE_A = (64 + DH_R) ** -0.5
SCALE_B = DH_B ** -0.5
SCALE_C = DH_C ** -0.5
NEG = -1e30
TAKEN = -3e38
TWO_PI = 2.0 * np.pi

RING = 7
SLOT = 3072
MODW = SLOT // KD
FC = 256
C_DENSE = F_DENSE // FC
C_EXP = F_EXP // FC
MOD_SLOTS = 3 * D // MODW
PROJ = [312, 384, 320, 384, 384, 384, 384, 384, 384, 256]
OFF = dict(qn=0, qr=256, ckv=384, kr=512, iq=544, ik=800, iw=864, mq=868, mk=1380, mv=1892, mi=2404,
           mf=2408, mo=2412, nq=2924, nkc=3180, nvc=3244, nks=3308, nvs=3372, nkw=3436, nvw=3500, ng=3564)
PICK = [("qr", 0, 128), ("kr", 0, 32), ("ckv", 0, 128), ("iw", 0, 4), ("mi", 0, 4), ("mf", 0, 4), ("ng", 0, 12),
        ("iq", 0, 256), ("nvs", 0, 64), ("nvw", 0, 64), ("ik", 0, 64), ("qn", 0, 256),
        ("nkc", 0, 64), ("nvc", 0, 64), ("nks", 0, 64), ("nkw", 0, 64), ("nq", 0, 256), ("mq", 0, 512),
        ("mk", 0, 512), ("mv", 0, 512), ("mo", 0, 512)]
LW_W2, LW_UK, LW_UV, LW_CW, LW_CB, LW_POS, LW_END = 0, 128, 384, 640, 672, 680, 712

UNITS = [("A", 0), ("A", 1), ("S", 0), ("S", 1), ("W", 0), ("W", 1)]
START = [range(6), range(24, 26)]
FILL = [[(6, 7), (8, 9), (10, 11, 12), (13, 14), (15, 16, 17), (18, 19), (20, 21), (22, 23)],
        [(26,), (27,), (), (28,), (), (29,), (30,), (31,)]]


def row_steps(rows, pending, last=False):
    steps = []
    for i in rows:
        steps.append(("part", i))
        if pending is not None:
            steps.append(("row", pending))
        pending = i
    if last:
        steps.append(("row", pending))
        pending = None
    return steps, pending


def fill_steps(l):
    pending, out = None, []
    for n, rows in enumerate(FILL[l]):
        steps, pending = row_steps(rows, pending, n == len(FILL[l]) - 1)
        out.append(steps)
    return out


def plan_jobs():
    jobs = []

    def next_bank(b):
        while len(jobs) % 8 != b:
            jobs.append(None)

    for l in range(DEPTH):
        next_bank(0)
        jobs += row_steps(START[l], None, True)[0]
        jobs += [("uT", l, 0, 0, k) for k in range(2)]
        if l > 0:
            next_bank(0)
        jobs.append(("A1_0", l))
        jobs += [("uT", l, 0, 1, k) for k in range(2)]
        jobs += [(n, l) for n in ("A1_1", "iq", "A2", "ik", "qn", "kv", "nq", "gT", "mqk0", "mqk1",
                                  "lgE0", "lgO0", "lgE1", "lgO1", "mqk2", "mqk3", "ropeT", "ckvT",
                                  "mv0", "mv1", "vo0", "vo1", "mo", "cmpp", "qabsE", "qabsO", "cmph",
                                  "cmpkv", "cS")]
        for n in range(len(UNITS) + 1):
            if n < len(UNITS):
                jobs += [("sc", l, n, 0), ("sc", l, n, 1)]
                jobs += fill_steps(l)[n]
            if n == 0:
                jobs += [("PcT", l), ("oC", l)]
            if n >= 1:
                kind, t = UNITS[n - 1]
                jobs += [("PT", l, n - 1, k) for k in range(t + 1)]
                if kind == "A":
                    jobs.append(("ol", l, n - 1))
                jobs.append(("o", l, n - 1))
        jobs += [("Mb0", l), ("Mb1", l), ("cT", l)]
        jobs += [("sM", l, h) for h in range(HEADS)]
        jobs += fill_steps(l)[6]
        next_bank(4)
        jobs += [("hM", l, t, p) for t in range(2) for p in range(2)]
        jobs += fill_steps(l)[7]
        next_bank(0)
        for t in range(2):
            jobs += [("yT", l, t, k) for k in range(2)]
            jobs += [("out", l, t, h) for h in range(2)]
        jobs += [("uT", l, 1, t, k) for t in range(2) for k in range(2)]
    return jobs


def plan_ring():
    ring = []
    for l in range(DEPTH):
        ring += [("mod", 0, i * SLOT, SLOT, ("part", i)) for i in START[l]]
        last = ["A1_1", "A2", "qn", "nq", "mqk1", "mqk2", "mqk3", "mv1", "vo1", "mo"]
        at = 0
        for w, j in zip(PROJ, last):
            ring.append(("in", l, at * KD, w * KD, (j, l)))
            at += w
        ring += [("w1", l, j * 2048, 2048, ("cmpp", l)) for j in range(2)]
        for rows in FILL[l]:
            ring += [("mod", 0, i * SLOT, SLOT, ("part", i)) for i in rows]
        ring += [("out", l, a * D, (b - a) * D, ("out", l, 1, 1)) for a, b in ((0, 3), (3, 6), (6, 8))]
        if l == 0:
            ring += [("ffn", 0, i * SLOT, SLOT, i // 2) for i in range(2 * C_DENSE)]
    return ring


JOBS = plan_jobs()
SLOTS = plan_ring()
MOE0 = len(SLOTS)
assert MOE0 % RING == 0 and (2 * C_EXP) % RING == 0


def build_trunk(nc, dram, out):
    place, uses = {}, [0] * 8
    for i, name in enumerate(JOBS):
        if name is not None:
            place[name] = (i % 8, uses[i % 8])
            uses[i % 8] += 1
    slot_of = {}
    for n, (arr, l, col, w, _) in enumerate(SLOTS):
        slot_of.setdefault((arr, l), []).append(n)

    with ExitStack() as ctx:
        def sb(name, shape, dt=F32):
            return ctx.enter_context(nc.sbuf_tensor(name, shape, dt))

        sems = {}

        def S(name):
            if name not in sems:
                sems[name] = ctx.enter_context(nc.semaphore(name))
            return sems[name]

        ring = sb("ring", [P, RING, SLOT])
        x = sb("x", [P, TILES, D])
        u = sb("u", [P, TILES, D])
        uT = sb("uT", [P, KD, T])
        mods = sb("mods", [P, 3, D])
        modss, modg = mods[:, 0:2, :], mods[:, 2, :]
        gn = sb("gn", [P, D])
        kvn = sb("kvn", [P, D_C])
        lw = sb("lw", [P, LW_END])
        raw = sb("raw", [P, 8 * (T + 3)])
        rawv = raw[:, :].rearrange("p (b t) -> p b t", b=8)
        lnp = raw[:, 0:2 * D].rearrange("p (a n) -> p a n", a=2)
        ident = sb("ident", [P, P])
        cm = sb("cm", [P, T])
        cmT = sb("cmT", [P, T])
        cmpa = sb("cmpa", [P, TILES, N_CMP])
        cmpm = sb("cmpm", [P, TILES, N_CMP])
        ccol = sb("ccol", [P, KD])
        csil = sb("csil", [P, KD])
        bmod = sb("bmod", [P, MODW])
        rowst = sb("rowst", [P, MODW])
        quarter = sb("quarter", [P, 1])
        pos = sb("pos", [P, TILES], I32)
        ang = sb("ang", [P, TILES, 16])
        ang2 = sb("ang2", [P, TILES, 16])
        sn = sb("sn", [P, TILES, 16])
        cs = sb("cs", [P, TILES, 16])
        freq = sb("freq", [P, 16])
        A1 = sb("A1", [P, TILES, 312])
        A2 = sb("A2", [P, TILES, P])
        rot = sb("rot", [P, TILES, 8, DH_R])
        rtmp = sb("rtmp", [P, TILES, 5, 16])
        ropeT = sb("ropeT", [P, 3, T])
        ones, before = ropeT[:, 0, 0:P], ropeT[:, 1, 0:P]
        ckvn = sb("ckvn", [P, TILES, D_C])
        ckvT = sb("ckvT", [P, T])
        ik2 = sb("ik2", [P, T])
        kc2 = sb("kc2", [P, 2, T])
        ks2 = sb("ks2", [P, T])
        kw2 = sb("kw2", [P, T])
        blk = sb("blk", [P, 2 * 16 * 16 + 16])
        blocks = blk[:, 0:512].rearrange("p (j c n) -> p j c n", j=2, c=16)[:, :, :, 0:N_CMP]
        stack = sb("stack", [P, 16])
        r3 = sb("r3", [P, 2560])
        iqT = r3[:, 0:512].rearrange("p (b t) -> p b t", b=2)
        qnT = r3[:, 512:1024].rearrange("p (b t) -> p b t", b=2)
        nqT = r3[:, 1024:1536].rearrange("p (b t) -> p b t", b=2)
        qabsT = r3[:, 1536:2560].rearrange("p (h t) -> p h t", h=4)
        partst = r3[:, 0:1024].rearrange("p (i n) -> p i n", i=2)[:, :, 0:MODW]
        gwT = r3[:, 0:512].rearrange("p (j t) -> p j t", j=2)
        hbuf = r3[:, 512:1024].rearrange("p (j f) -> p j f", j=2)
        sgb = r3[:, 1024:1536].rearrange("p (j f) -> p j f", j=2)
        hT = r3[:, 1536:2048].rearrange("p (j b s) -> p j b s", j=2, b=2)
        prob = sb("prob", [P, 2, HEADS, T])
        yacc = prob[:, :, :, :].rearrange("p a h t -> p a (h t)")
        r2 = sb("r2", [P, 3072])
        PTs = r2[:, 0:1024].rearrange("p (k n) -> p k n", k=2)
        rel = r2[:, 0:1024].rearrange("p (h t) -> p h t", h=4)
        cmps = r2[:, 1024:1280]
        olT = r2[:, 1024:1536].rearrange("p (h t) -> p h t", h=4)
        Dm = r2[:, 1536:3072].rearrange("p (h t) -> p h t", h=4)
        oe = r2[:, 0:2048].rearrange("p (j n) -> p j n", j=2)
        gsel = r2[:, 2048:2560].rearrange("p (t s) -> p t s", t=2)
        gwsel = r2[:, 2560:3072].rearrange("p (t s) -> p t s", t=2)
        score = sb("score", [P, TILES, T])
        iota, iotai = score[:, 0, :], score[:, 1, :].bitcast(I32)
        mvt = sb("mvt", [P, TILES, HEADS, DH_B + 1])
        mog = sb("mog", [P, TILES, 512])
        ct = sb("ct", [P, 2, T])
        rows = modss[0:HEADS, :, :].rearrange("p a n -> p (a n)")
        gi, gf, lse, crow, brow = (rows[:, i * T:(i + 1) * T] for i in range(5))
        scanA, scanB = (rows[:, 5 * T + i * (P + T):5 * T + (i + 1) * (P + T)] for i in range(2))
        gbt = sb("gbt", [HEADS, 2])
        ccl = sb("ccl", [P, 8])
        emc = sb("emc", [P, 8])
        hid = sb("hid", [P, 2, N_CMP])
        kcmp = sb("kcmp", [P, 2, N_CMP])
        vbd = sb("vbd", [P, HEADS, DH_C])
        Pc = sb("Pc", [P, TILES, HEADS, 32])
        PcT = rot[:, 0, :, :].rearrange("p h r -> p (h r)")
        gates = sb("gates", [P, TILES, 12])
        mx = sb("mx", [P, 6, HEADS])
        rs = sb("rs", [P, 6, HEADS])
        st8 = sb("st8", [P, TILES, HEADS])
        st8b = sb("st8b", [P, TILES, HEADS])
        max8 = sb("max8", [P, 8])
        dn = sb("dn", [P, 4])
        ss = sb("ss", [P, TILES, 12])
        rstd = sb("rstd", [P, TILES, 12])
        kvs = sb("kvs", [P, 4])
        bst = sb("bst", [P, TILES, 2, 6])
        mv2 = sb("mv2", [P, TILES, 2])
        lsd = sb("lsd", [P, TILES])
        eps5 = sb("eps5", [P, 1])
        eps6 = sb("eps6", [P, 1])
        router = sb("router", [P, KD, EXPERTS])
        lg = sb("lg", [P, TILES, EXPERTS])
        top8 = sb("top8", [P, TILES, EXPERTS])
        idx8 = sb("idx8", [P, TILES, EXPERTS], U32)
        idxf = sb("idxf", [P, TILES, EXPERTS])
        w12 = sb("w12", [P, TILES, 2])
        oh = sb("oh", [P, 2, TILES, EXPERTS])
        routed = sb("routed", [P, TILES, EXPERTS])
        table = sb("table", [P, 2 * TILES, EXPERTS])
        now = sb("now", [P, 2 * TILES])
        flag = sb("flag", [1, EXPERTS], I32)
        lsd8 = sb("lsd8", [1, EXPERTS])
        modrow = nc.dram_tensor("modrow", (2 * DEPTH, 3 * D), F32)

        ps = ctx.enter_context(nc.psum_tensor("ps", [P, 8, 512], F32))
        GU, TB, XB, ACC = 0, 2, 3, 4

        def bank(*job):
            return ps[:, place[job][0], :]

        def full(eng, *job):
            b, use = place[job]
            eng.wait_ge(S(f"bank_full{b}"), use + 1)

        def emptied(*job):
            return S(f"bank_free{place[job][0]}")

        def copied(eng, *job):
            b, use = place[job]
            eng.wait_ge(S(f"bank_free{b}"), use + 1)

        def slot_full(eng, n, more=0):
            eng.wait_ge(S(f"slot_full{n % RING}"), 16 * (n // RING + 1) + more)

        def by_rows(eng, kind, body):
            with eng.If(kind > 2):
                body(2 * P)
            with eng.Else():
                with eng.If(kind > 1):
                    body(P)
                with eng.Else():
                    with eng.If(kind > 0):
                        body(96)
                    with eng.Else():
                        body(64)
                    eng.nop()
                eng.nop()

        def chain(eng, name):
            count = [0]

            def link(ins):
                count[0] += 1
                ins.then_inc(S(name), 1)
                eng.wait_ge(S(name), count[0])
            return link

        for b in range(8):
            S(f"bank_full{b}")
            S(f"bank_free{b}")
        for b in range(RING):
            S(f"slot_full{b}")

        block = ctx.enter_context(nc.Block())

        @block.sync
        def _(sp):
            src = {"mod": dram["mod"], "in": dram["w_in"], "w1": dram["w1"], "out": dram["w_out"], "ffn": dram["ffn"]}
            sp.dma_start(ccol[:, :], dram["c"]).then_inc(S("c_in"), 16)

            def load(n):
                if n >= RING:
                    last = SLOTS[n - RING][4]
                    if isinstance(last, int):
                        sp.wait_ge(S("down_done"), last + 1)
                    else:
                        full(sp, *last)
                if n < MOE0:
                    arr, l, col, w, _ = SLOTS[n]
                    a = src[arr]
                    if arr in ("mod", "ffn"):
                        s = a[col // SLOT]
                    elif arr == "in":
                        s = a[l, col * P:(col + w) * P].rearrange("(p n) -> p n", p=P)
                    else:
                        s = a[l, :, col:col + w]
                    sp.dma_start(ring[:, n % RING, 0:w], s).then_inc(S(f"slot_full{n % RING}"), 16)
                else:
                    sp.dma_start(ring[:, n % RING, :], dram["moe"][n - MOE0]).then_inc(S(f"slot_full{n % RING}"), 16)

            for n in range(MOE0 + RING):
                load(n)
                if n == 1:
                    sp.dma_start(x[:, :, :], dram["x"].rearrange("(t p) n -> p t n", p=P)).then_inc(S("x_in"), 16)

            def load_expert(e, q):
                sp.wait_ge(S("down_done"), (q - RING) // 2 + 1 + C_DENSE + C_EXP * e)
                sp.dma_start(ring[:, q % RING, :],
                             dram["moe"][bass.ds(e * (2 * C_EXP) + q, 1)].rearrange("a p n -> p (a n)")
                             ).then_inc(S(f"slot_full{q % RING}"), 16)

            with sp.Fori(0, EXPERTS - 1) as e:
                for q in range(RING, 2 * C_EXP + RING):
                    load_expert(e, q)
            for q in range(RING, 2 * C_EXP):
                load_expert(EXPERTS - 1, q)
            for t in range(TILES):
                sp.wait_ge(S("x_done"), 2 * (2 * DEPTH - 1) + t + 1)
                sp.dma_start(out[t * P:(t + 1) * P, :], x[:, t, :]).then_inc(S("stored"), 16)
            sp.wait_ge(S("stored"), 16 * TILES)

        @block.gpsimd
        def _(pool):
            link = chain(pool, "pool_order")
            g = nc.gpsimd
            g.memset(bmod[:, :], 0.0)
            link(g.memset(ident[:, :], 0.0))
            g.dma_start(bmod[0:32, :], dram["b_mod"]).then_inc(S("bmod_in"), 16)
            g.affine_select(out=ident[:, :], in_=ident[:, :], compare_op=ALU.not_equal, fill=1.0, base=0,
                            pattern=[[-1, P]], channel_multiplier=1)
            link(g.memset(quarter[:, :], 0.0))
            for i in range(4):
                ins = g.affine_select(out=quarter[:, :], in_=quarter[:, :], compare_op=ALU.not_equal, fill=1.0,
                                      base=-32 * i, pattern=[[0, 1]], channel_multiplier=1)
                if i < 3:
                    link(ins)
            ins.then_inc(S("ident_ready"), 1)
            g.memset(cm[:, :], 0.0)
            g.memset(cmT[:, :], 0.0)
            g.memset(cmpa[:, :, :], 0.0)
            g.memset(cmpm[:, :, :], 1.0)
            g.memset(vbd[:, :, :], 0.0)
            g.memset(Pc[:, :, :, :], 0.0)
            g.memset(kcmp[:, :, :], 0.0)
            g.memset(blk[:, :], 0.0)
            g.memset(stack[:, :], 0.0)
            link(g.memset(mvt[:, :, :, DH_B:DH_B + 1], 1.0))
            g.affine_select(out=cm[:, P:T], in_=cm[:, P:T], compare_op=ALU.is_ge, fill=NEG, base=0,
                            pattern=[[-1, P]], channel_multiplier=1)
            g.affine_select(out=cmT[:, 0:P], in_=cmT[:, 0:P], compare_op=ALU.is_ge, fill=NEG, base=0,
                            pattern=[[1, P]], channel_multiplier=-1)
            for i in range(4):
                link(g.affine_select(out=stack[:, :], in_=stack[:, :], compare_op=ALU.not_equal, fill=1.0,
                                     base=-32 * i, pattern=[[-1, 16]], channel_multiplier=1))
            for m, fill in ((cmpa, NEG), (cmpm, 0.0)):
                ins = g.affine_select(out=m[:, :, :], in_=m[:, :, :], compare_op=ALU.is_ge, fill=fill, base=-31,
                                pattern=[[P, TILES], [-16, N_CMP]], channel_multiplier=1)
            ins.then_inc(S("consts"), 1)
            g.dma_start(pos[:, :], dram["positions"]).then_inc(S("pos_in"), 16)
            g.dma_start(freq[:, :], dram["inv_freq"].partition_broadcast(P)).then_inc(S("pos_in"), 16)
            g.dma_start(router[:, :, :], dram["router"]).then_inc(S("router_in"), 16)

            def load_small(l):
                g.dma_start(lw[:, :], dram["lw"][l]).then_inc(S("small_in"), 16)
                g.dma_start(gn[:, :], dram["grp_norm"][l].partition_broadcast(P)).then_inc(S("small_in"), 16)
                g.dma_start(kvn[:, :], dram["kv_norm"][l].partition_broadcast(P)).then_inc(S("small_in"), 16)
                g.dma_start(gbt[:, :], dram["gate_b"][l]).then_inc(S("small_in"), 16)

            def store_row(i):
                if i < MOD_SLOTS:
                    return
                copied(pool, "row", i)
                half, part = divmod(i, 8)
                r = 32 * (i % 4)
                g.dma_start(modrow[half:half + 1, part * MODW:(part + 1) * MODW],
                            rowst[r:r + 1, :]).then_inc(S(f"row_stored{i % 4}"), 16)

            def load_mod(half):
                for i in range(4):
                    pool.wait_ge(S(f"row_stored{i}"), 32 * half)
                pool.wait_ge(S("u_done"), 2 * half)
                g.dma_start(modss[:, :, :].rearrange("p a n -> p (a n)"),
                            modrow[half, 0:2 * D].partition_broadcast(P)).then_inc(S("modss_in"), 16)

            def load_gate(half):
                pool.wait_ge(S("z_done"), 2 * half)
                g.dma_start(modg[:, :], modrow[half, 2 * D:3 * D].partition_broadcast(P)
                            ).then_inc(S("modg_in"), 16)

            def load_ln(half):
                g.dma_start(lnp, dram["ln"][half].partition_broadcast(P)).then_inc(S("ln_in"), 16)

            def rope(l):
                copied(pool, "A1_1", l)
                if l == 0:
                    pool.wait_ge(S("angles"), 1)
                if l > 0:
                    full(pool, "ropeT", l - 1)
                v = A1[:, :, 0:160].rearrange("p t (h r) -> p t h r", h=5)
                c5 = cs[:, :, :].unsqueeze(2).broadcast_to([P, TILES, 5, 16])
                s5 = sn[:, :, :].unsqueeze(2).broadcast_to([P, TILES, 5, 16])
                o1, o2 = rot[:, :, 0:5, 0:16], rot[:, :, 0:5, 16:32]
                g.tensor_tensor(o1, v[:, :, :, 0:16], c5, ALU.mult)
                link(g.tensor_tensor(rtmp[:, :, :, :], v[:, :, :, 16:32], s5, ALU.mult))
                g.tensor_tensor(o1, o1, rtmp[:, :, :, :], ALU.subtract)
                link(g.tensor_tensor(o2, v[:, :, :, 0:16], s5, ALU.mult))
                link(g.tensor_tensor(rtmp[:, :, :, :], v[:, :, :, 16:32], c5, ALU.mult))
                link(g.tensor_tensor(o2, o2, rtmp[:, :, :, :], ALU.add))
                for t in range(TILES):
                    last = g.tensor_copy(rot[:, t, 5:8, :], rot[:, t, 4:5, :].broadcast_to([P, 3, DH_R]))
                last.then_inc(S("rope_done"), 1)

            def gate_scans(l):
                pool.wait_ge(S("lse_done"), l + 1)
                g.memset(scanA[:, 0:P], 0.0)
                g.memset(scanB[:, 0:P], 0.0)
                a, b = scanA[:, P:P + T], scanB[:, P:P + T]
                link(g.tensor_scalar(brow[:, :], gf[:, :], 0.0, None, ALU.min))
                link(g.tensor_tensor(a, brow[:, :], lse[:, :], ALU.subtract))

                src, dst = scanA, scanB
                for d in SHIFTS:
                    link(g.tensor_tensor(dst[:, P:P + T], src[:, P:P + T], src[:, P - d:P + T - d], ALU.add))
                    src, dst = dst, src
                g.tensor_copy(brow[:, :], a)
                link(g.tensor_tensor(crow[:, :], gi[:, :], a, ALU.subtract))
                g.tensor_copy(b, crow[:, :]).then_inc(S("sums_done"), 1)

            load_small(0)
            for l in range(DEPTH):
                if l:
                    load_mod(2 * l)
                    load_gate(2 * l)
                    for i in START[l]:
                        store_row(i)
                    pool.wait_ge(S("x_done"), 4 * l)
                g.memset(rawv[:, :, 0:3], 0.0).then_inc(S("raw_padded"), 1)
                rope(l)
                gate_scans(l)
                for rows in FILL[l]:
                    for i in rows:
                        store_row(i)
                full(pool, "cT", l)
                load_mod(2 * l + 1)
                full(pool, "sM", l, 3)
                load_ln(2 * l)
                load_gate(2 * l + 1)
                pool.wait_ge(S("x_done"), 4 * l + 2)
                load_ln(2 * l + 1)
                if l + 1 < DEPTH:
                    load_small(l + 1)
            link(g.iota(iotai, pattern=[[1, T]], base=0, channel_multiplier=0))
            link(g.tensor_copy(iota, iotai))
            g.memset(ones, 1.0)
            link(g.memset(before, 1.0))
            g.affine_select(out=before, in_=before, compare_op=ALU.is_gt, fill=0.0, base=0,
                            pattern=[[1, P]], channel_multiplier=-1).then_inc(S("iota_ready"), 1)

        @block.tensor
        def _(pe):
            order = iter([job for job in JOBS if job is not None])
            mm = nc.tensor.matmul
            tr = nc.tensor.transpose

            def begin(*job):
                assert next(order) == job, job
                b, use = place[job]
                if use:
                    pe.wait_ge(S(f"bank_free{b}"), use)
                return ps[:, b, :]

            def end(ins, *job):
                ins.then_inc(S(f"bank_full{place[job][0]}"), 1)

            waited = set()

            def weights(arr, l, i):
                n = slot_of[arr, l][i]
                if n not in waited:
                    slot_full(pe, n)
                    waited.add(n)
                return ring[:, n % RING, :]

            def part(i):
                o = begin("part", i)
                w = weights("mod", 0, i).rearrange("p (k n) -> p k n", k=KD)
                for k in range(KD):
                    r = 32 * (k % 4)
                    mm(o[r:r + 32, 0:MODW], csil[:, k:k + 1].broadcast_to([P, 32]), w[:, k, :],
                       start=(k < 4), stop=(k >= 4 and k % 4 != (i + 1) % 4))
                if i == 0:
                    pe.wait_ge(S("ident_ready"), 1)
                    pe.wait_ge(S("bmod_in"), 16)
                r = 32 * ((i + 1) % 4)
                end(mm(o[r:r + 32, 0:MODW], ident[:, i:i + 1].broadcast_to([P, 32]), bmod[:, :],
                       start=False, stop=True), "part", i)

            def row(i):
                o = begin("row", i)
                copied(pe, "part", i)
                a, m = (0, P) if i < MOD_SLOTS else (32 * (i % 4), 1)
                end(mm(o[a:a + m, 0:MODW], quarter[:, :].broadcast_to([P, m]), partst[:, i % 2, :],
                       start=True, stop=True), "row", i)

            def fill(steps):
                for what, i in steps:
                    (part if what == "part" else row)(i)

            def transposes(name, *tag):
                t = tag[-1]
                for kk in range(2):
                    o = begin(name, *tag, kk)
                    for i in range(4):
                        k = 4 * kk + i
                        ins = tr(o[:, i * P:(i + 1) * P], u[:, t, k * P:(k + 1) * P], ident[:, :])
                    end(ins, name, *tag, kk)

            def proj_rows(o, w, a, b, t):
                for k in range(KD):
                    ins = mm(o, uT[:, k, t * P:(t + 1) * P], w[:, k, a:b], start=(k == 0), stop=(k == KD - 1))
                return ins

            def proj_cols(o, w, a, b):
                for k in range(KD):
                    ins = mm(o, w[:, k, a:b], uT[:, k, :], start=(k == 0), stop=(k == KD - 1))
                return ins

            def two_halves(jobs, product):
                banks = [begin(*job) for job in jobs]
                for i in range(2):
                    for odd, job in enumerate(jobs):
                        ins = product(banks[odd], slice(64 * odd, 64 * odd + 64), i)
                        if i == 1:
                            end(ins, *job)

            def mixer(l):
                if l == 0:
                    pe.wait_ge(S("csil_done"), 1)
                fill(row_steps(START[l], None, True)[0])

                def win(i):
                    return weights("in", l, i)[:, 0:KD * PROJ[i]].rearrange("p (k n) -> p k n", k=KD)

                w = win(0)
                for t in range(2):
                    pe.wait_ge(S("u_done"), 4 * l + t + 1)
                    transposes("uT", l, 0, t)
                    copied(pe, "uT", l, 0, t, 1)
                    o = begin(f"A1_{t}", l)
                    end(proj_rows(o[:, 0:312], w, 0, 312, t), f"A1_{t}", l)
                w = win(1)
                o = begin("iq", l)
                for b in range(2):
                    ins = proj_cols(o[:, b * T:(b + 1) * T], w, b * P, (b + 1) * P)
                end(ins, "iq", l)
                o = begin("A2", l)
                for t in range(2):
                    ins = proj_rows(o[:, t * P:(t + 1) * P], w, 256, 384, t)
                end(ins, "A2", l)
                w = win(2)
                o = begin("ik", l)
                end(proj_cols(o[0:64, 0:T], w, 0, 64), "ik", l)
                o = begin("qn", l)
                for b in range(2):
                    ins = proj_cols(o[:, b * T:(b + 1) * T], w, 64 + b * P, 64 + (b + 1) * P)
                end(ins, "qn", l)
                w = win(3)
                o = begin("kv", l)
                for b in range(2):
                    ins = proj_cols(o[:, b * T:(b + 1) * T], w, b * P, (b + 1) * P)
                end(ins, "kv", l)
                o = begin("nq", l)
                proj_cols(o[:, 0:T], w, 256, 384)
                w = win(4)
                end(proj_cols(o[:, T:2 * T], w, 0, P), "nq", l)
                o = begin("gT", l)
                copied(pe, "A1_1", l)
                for a in range(2):
                    for t in range(2):
                        ins = tr(o[0:4, (2 * a + t) * P:(2 * a + t + 1) * P], A1[:, t, 292 + 4 * a:296 + 4 * a],
                                 ident[:, :])
                end(ins, "gT", l)

                def mqk(i):
                    o = begin(f"mqk{i}", l)
                    for j in range(2):
                        b = 2 * i + j + 1
                        ins = proj_cols(o[:, j * T:(j + 1) * T], win(4 + b // 3), (b % 3) * P, (b % 3 + 1) * P)
                    end(ins, f"mqk{i}", l)
                mqk(0)
                mqk(1)
                copied(pe, "iq", l)
                copied(pe, "ik", l)
                for t in range(2):
                    n = (t + 1) * P
                    two_halves([(f"lgE{t}", l), (f"lgO{t}", l)],
                               lambda o, r, i: mm(o[:, i * T:i * T + n], iqT[r, i, t * P:(t + 1) * P], ik2[r, 0:n],
                                                  start=True, stop=True))
                mqk(2)
                mqk(3)
                o = begin("ropeT", l)
                pe.wait_ge(S("rope_done"), l + 1)
                for a in range(2):
                    for t in range(2):
                        ins = tr(o[:, (2 * a + t) * P:(2 * a + t + 1) * P],
                                 rot[:, t, 4 * a:4 * a + 4, :].rearrange("p h r -> p (h r)"), ident[:, :])
                end(ins, "ropeT", l)
                o = begin("ckvT", l)
                pe.wait_ge(S("ckvn_done"), l + 1)
                for t in range(2):
                    ins = tr(o[:, t * P:(t + 1) * P], ckvn[:, t, :], ident[:, :])
                end(ins, "ckvT", l)
                w = win(7)
                for t in range(2):
                    o = begin(f"mv{t}", l)
                    end(proj_rows(o[:, 0:384], w, 0, 384, t), f"mv{t}", l)
                w = win(8)
                for t in range(2):
                    o = begin(f"vo{t}", l)
                    end(proj_rows(o[:, 0:384], w, 0, 384, t), f"vo{t}", l)
                w = win(9)
                o = begin("mo", l)
                for t in range(2):
                    ins = proj_rows(o[:, t * 256:(t + 1) * 256], w, 0, 256, t)
                end(ins, "mo", l)
                o = begin("cmpp", l)
                pe.wait_ge(S("blk_done"), l + 1)
                for j in range(2):
                    w = weights("w1", l, j)
                    for c in range(16):
                        r, at = 32 * (c % 4), (16 * j + c) * 16
                        ins = mm(o[r:r + 32, j * P:(j + 1) * P], blk[:, at:at + 32], w[:, c * P:(c + 1) * P],
                                 start=(c < 4), stop=(c >= 12))
                end(ins, "cmpp", l)
                copied(pe, "qn", l)
                pe.wait_ge(S("small_in"), 64 * (l + 1))
                two_halves([("qabsE", l), ("qabsO", l)],
                           lambda o, r, i: mm(o[:, i * T:(i + 1) * T], lw[r, LW_UK + i * P:LW_UK + (i + 1) * P],
                                              qnT[r, i, :], start=True, stop=True))
                o = begin("cmph", l)
                copied(pe, "cmpp", l)
                for j in range(2):
                    ins = mm(o[:, j * N_CMP:(j + 1) * N_CMP], cmps[:, j * P:(j + 1) * P], stack[:, 0:N_CMP],
                             start=True, stop=True)
                end(ins, "cmph", l)
                o = begin("cmpkv", l)
                copied(pe, "cmph", l)
                mm(o[0:64, 0:N_CMP], lw[:, LW_W2:LW_W2 + 64], hid[:, 0, :], start=True, stop=True)
                end(mm(o[0:N_CMP, 64:128], hid[:, 1, :], lw[:, LW_W2 + 64:LW_W2 + 128], start=True, stop=True),
                    "cmpkv", l)
                o = begin("cS", l)
                copied(pe, "nq", l)
                copied(pe, "cmpkv", l)
                for t in range(2):
                    for i in range(2):
                        c = (2 * t + i) * 2 * N_CMP
                        ins = mm(o[:, c:c + 2 * N_CMP], nqT[:, i, t * P:(t + 1) * P],
                                 kcmp[:, :, :].rearrange("p a n -> p (a n)"), start=True, stop=True)
                end(ins, "cS", l)

                def scores(n):
                    kind, t = UNITS[n]
                    m = (t + 1) * P
                    if kind == "A" and t == 0:
                        copied(pe, "qabsO", l)
                        copied(pe, "ropeT", l)
                        copied(pe, "ckvT", l)
                    if n == 2:
                        copied(pe, "kv", l)
                        copied(pe, "A2", l)
                    if kind != "A":
                        keys = ks2 if kind == "S" else kw2
                        two_halves([("sc", l, n, part) for part in range(2)],
                                   lambda o, r, i: mm(o[:, i * T:i * T + m], nqT[r, i, t * P:(t + 1) * P],
                                                      keys[r, 0:m], start=True, stop=True))
                        return
                    for part in range(2):
                        o = begin("sc", l, n, part)
                        for i in range(2):
                            h = part + 2 * i
                            mm(o[:, i * T:i * T + m], qabsT[:, h, t * P:(t + 1) * P], ckvT[:, 0:m],
                               start=True, stop=False)
                            r = slice(64 * part, 64 * part + 32)
                            ins = mm(o[:, i * T:i * T + m], ropeT[r, i, t * P:(t + 1) * P], ropeT[r, 2, 0:m],
                                     start=False, stop=True)
                        end(ins, "sc", l, n, part)

                def attend(n):
                    kind, t = UNITS[n]
                    pe.wait_ge(S("exp_done"), 6 * l + n + 1)
                    for kb in range(t + 1):
                        o = begin("PT", l, n, kb)
                        for h in range(HEADS):
                            ins = tr(o[:, h * P:(h + 1) * P], prob[:, n % 2, h, kb * P:(kb + 1) * P], ident[:, :])
                        end(ins, "PT", l, n, kb)
                    if kind == "A":
                        o = begin("ol", l, n)
                        copied(pe, "PT", l, n, t)
                        for kb in range(t + 1):
                            ins = mm(o[:, :], ckvn[:, kb, :], PTs[:, kb, :], start=(kb == 0), stop=(kb == t))
                        end(ins, "ol", l, n)
                        o = begin("o", l, n)
                        copied(pe, "ol", l, n)
                        for h in range(HEADS):
                            hh = ORDER[h]
                            ins = mm(o[:, h * 64:(h + 1) * 64], olT[:, h, :],
                                     lw[:, LW_UV + hh * 64:LW_UV + (hh + 1) * 64], start=True, stop=True)
                        end(ins, "o", l, n)
                    else:
                        o = begin("o", l, n)
                        copied(pe, "PT", l, n, t)
                        c = 0 if kind == "S" else 64
                        for h in range(HEADS):
                            hh = ORDER[h]
                            for kb in range(t + 1):
                                ins = mm(o[:, hh * 64:(hh + 1) * 64], PTs[:, kb, h * P:(h + 1) * P],
                                         A2[:, kb, c:c + 64], start=(kb == 0), stop=(kb == t))
                        end(ins, "o", l, n)

                for n in range(len(UNITS) + 1):
                    if n < len(UNITS):
                        scores(n)
                        fill(fill_steps(l)[n])
                    if n == 0:
                        o = begin("PcT", l)
                        pe.wait_ge(S("Pc_done"), l + 1)
                        for t in range(2):
                            ins = tr(o[:, t * P:(t + 1) * P], Pc[:, t, :, :].rearrange("p h n -> p (h n)"), ident[:, :])
                        end(ins, "PcT", l)
                        o = begin("oC", l)
                        copied(pe, "PcT", l)
                        for t in range(2):
                            ins = mm(o[:, t * 256:(t + 1) * 256], PcT[:, t * P:(t + 1) * P],
                                     vbd[:, :, :].rearrange("p h d -> p (h d)"), start=True, stop=True)
                        end(ins, "oC", l)
                    if n >= 1:
                        attend(n - 1)

                pe.wait_ge(S("scans_done"), l + 1)
                for p in range(2):
                    o = begin(f"Mb{p}", l)
                    for i in range(2):
                        h = 2 * p + i
                        ins = mm(o[:, i * T:(i + 1) * T], ident[0:HEADS, h:h + 1].broadcast_to([HEADS, P]),
                                 scanB[:, P:P + T], start=True, stop=True)
                    end(ins, f"Mb{p}", l)
                o = begin("cT", l)
                for a, r in enumerate((crow, brow)):
                    for t in range(2):
                        c = 8 * a + 4 * t
                        ins = tr(o[:, c:c + 4], r[:, t * P:(t + 1) * P], ident[0:4, 0:4])
                end(ins, "cT", l)
                pe.wait_ge(S("conv_done"), 8 * (l + 1))
                for h in range(HEADS):
                    o = begin("sM", l, h)
                    q, k = rawv[:, h, 3:3 + T], rawv[:, 4 + h, 3:3 + T]
                    mm(o[:, 0:T], k[:, 0:P], q, start=True, stop=True)
                    end(mm(o[:, T:T + P], k[:, P:T], q[:, P:T], start=True, stop=True), "sM", l, h)
                fill(fill_steps(l)[6])
                copied(pe, "vo1", l)
                for t in range(2):
                    for p in range(2):
                        o = begin("hM", l, t, p)
                        copied(pe, "sM", l, 2 * p + 1)
                        for i in range(2):
                            h = 2 * p + i
                            for kb in range(t + 1):
                                a = t * P if kb == 0 else T
                                ins = mm(o[:, i * 129:(i + 1) * 129], Dm[:, h, a:a + P], mvt[:, kb, h, :],
                                         start=(kb == 0), stop=(kb == t))
                        end(ins, "hM", l, t, p)
                fill(fill_steps(l)[7])

                for t in range(2):
                    pe.wait_ge(S("y_done"), 2 * l + t + 1)
                    transposes("yT", l, t)
                    copied(pe, "yT", l, t, 1)
                    for half in range(2):
                        o = begin("out", l, t, half)
                        for k in range(KD):
                            w = weights("out", l, k // 3)
                            c = (k % 3) * D + half * 512
                            ins = mm(o[:, :], uT[:, k, t * P:(t + 1) * P], w[:, c:c + 512],
                                     start=(k == 0), stop=(k == KD - 1))
                        end(ins, "out", l, t, half)
                pe.wait_ge(S("u_done"), 4 * l + 3)
                transposes("uT", l, 1, 0)

            def logits(t):
                for k in range(KD):
                    ins = mm(ps[:, ACC, t * 8:(t + 1) * 8], uT[:, k, t * P:(t + 1) * P], router[:, k, :],
                             start=(k == 0), stop=(k == KD - 1))
                return ins

            def second_tile(l):
                pe.wait_ge(S("u_done"), 4 * l + 4)
                transposes("uT", l, 1, 1)
                last_use = {}
                for job in JOBS[:JOBS.index(("uT", l, 1, 1, 1)) + 1]:
                    if job is not None:
                        last_use[place[job][0]] = job
                for job in last_use.values():
                    copied(pe, *job)

            def swiglu(rows, chunks, first, slots, after_first=None, between=None):
                n0, more = slots
                blocks = rows // P

                def gate_up(c):
                    for j in range(blocks):
                        for k in range(KD):
                            w = ring[:, (n0 + 2 * c + k // 4) % RING, (k % 4) * 512:(k % 4 + 1) * 512]
                            ins = mm(ps[:, GU + j, :], uT[:, k, j * P:(j + 1) * P], w,
                                     start=(k == 0), stop=(k == KD - 1))
                        if c == 0 and j == 0 and between:
                            between()
                    for a, m, o in ((0, 64, GU), (64, 32, GU + 1)):
                        if a < rows < P:
                            for k in range(KD):
                                w = ring[:, (n0 + 2 * c + k // 4) % RING, (k % 4) * 512:(k % 4 + 1) * 512
                                         ].rearrange("p (a f) -> p a f", a=2)
                                for i in range(P // m):
                                    ins = mm(ps[m * i:m * i + m, o, 0:4 * m], uT[:, k, a:a + m],
                                             w[:, :, 2 * m * i:2 * m * (i + 1)], start=(k == 0), stop=(k == KD - 1))
                    ins.then_inc(S("gu_filled"), 1)

                def turn_hidden():
                    if rows < P:
                        ins = tr(ps[:, TB, 0:P], hbuf[:, 0, 0:P], ident[:, :])
                        if rows == 96:
                            ins = tr(ps[0:64, TB, P:2 * P], hbuf[:, 1, 0:64], ident[:, :])
                    else:
                        for j, b in BLOCKS[blocks]:
                            ins = tr(ps[:, TB, (2 * j + b) * P:(2 * j + b + 1) * P],
                                     hbuf[:, j, b * P:(b + 1) * P], ident[:, :])
                    ins.then_inc(S("hT_filled"), 1)

                def down(c):
                    def w(b, half):
                        return ring[:, (n0 + 2 * c + b) % RING, 2048 + half * 512:2560 + half * 512]

                    begins, ends = c == 0, c == chunks - 1
                    for j in range(blocks):
                        for b in range(2):
                            for half in range(2):
                                ins = mm(ps[:, ACC + 2 * j + half, :], hT[:, j, b, :], w(b, half),
                                         start=(begins and b == 0), stop=(ends and b == 1))
                        if j == 0 and ends and between:
                            ins.then_inc(S("first_block_done"), 1)
                    if rows < P:
                        for half in range(2):
                            for b in range(2):
                                ins = mm(ps[64 * b:64 * b + 64, ACC + half, :], hT[:, 0, 0, 64 * b:64 * b + 64],
                                         w(b, half), start=begins, stop=ends)
                    if rows == 96:
                        for half in range(2):
                            for b in range(2):
                                q = 32 * (2 * half + b)
                                ins = mm(ps[q:q + 32, ACC + 2, :], hT[:, 1, b, 0:32], w(b, half),
                                         start=begins, stop=ends)
                    ins.then_inc(S("down_done"), 1)

                for c in range(chunks + 1):
                    if c > 0:
                        pe.wait_ge(S("h_ready"), first + c)
                        turn_hidden()
                    if c < chunks:
                        for i in range(2):
                            slot_full(pe, n0 + 2 * c + i, more)
                        gate_up(c)
                        if c == 0 and after_first:
                            after_first()
                    if c > 0:
                        pe.wait_ge(S("hT_ready"), first + c)
                        down(c - 1)

            def gather(e, n):
                pe.wait_ge(S("sel_ready"), e + 1)
                for kp in range(4):
                    for i in range(2):
                        k = 2 * kp + i
                        for t in range(TILES):
                            ins = mm(ps[:, kp, i * T:i * T + n], u[:, t, k * P:(k + 1) * P],
                                     gsel[:, t, 0:n], start=(t == 0), stop=(t == 1))
                    ins.then_inc(S("gather_filled"), 1)

            def expert(e, rows):
                def turn_weights():
                    groups = {64: [(0, 64)], 96: [(0, 64), (64, 32)], P: [(0, P)], 2 * P: [(0, P), (P, P)]}
                    for i, (a, m) in enumerate(groups[rows]):
                        for t in range(TILES):
                            ins = tr(ps[0:m, XB, i * T + t * P:i * T + (t + 1) * P], gwsel[:, t, a:a + m], ident[:, :])
                    ins.then_inc(S("gwT_filled"), 1)

                pe.wait_ge(S("gather_ready"), 4 * e + 4)
                pe.wait_ge(S("y_added"), 4 * e + 1)
                swiglu(rows, C_EXP, C_EXP * e + C_DENSE, (MOE0, 16 * (2 * C_EXP // RING) * e), turn_weights)

            def scatter(e, rows, last=False):
                pe.wait_ge(S("gwT_ready"), e + 1)
                pe.wait_ge(S("oe_ready"), e + 1)
                for t in range(TILES):
                    for half in range(2):
                        if not last:
                            pe.wait_ge(S("gather_ready"), 4 * e + 4 + 2 * t + half + 1)
                        c, o = slice(t * P, (t + 1) * P), ps[:, 2 * t + half, :]
                        ins = mm(o, gwT[:, 0, c], oe[:, 0, half * 512:(half + 1) * 512],
                                 start=True, stop=(rows in (64, P)))
                        if rows == 2 * P:
                            ins = mm(o, gwT[:, 1, c], oe[:, 1, half * 512:(half + 1) * 512], start=False, stop=True)
                        if rows == 96:
                            r = slice(64 * half, 64 * half + 64)
                            ins = mm(o, gwT[r, 1, c], oe[r, 1, 0:512], start=False, stop=True)
                        ins.then_inc(S("scatter_filled"), 1)

            mixer(0)
            copied(pe, "uT", 0, 1, 0, 1)
            swiglu(2 * P, C_DENSE, 0, (slot_of["ffn", 0][0], 0), between=lambda: second_tile(0))
            mixer(1)
            pe.wait_ge(S("router_in"), 16)
            copied(pe, "uT", 1, 1, 0, 1)
            assert place["yT", 1, 1, 0][0] == ACC
            copied(pe, "yT", 1, 1, 0)
            logits(0)
            second_tile(1)
            logits(1).then_inc(S("logits_filled"), 1)
            pe.wait_ge(S("routed_done"), 1)
            mm(ps[:, TB, 0:8], before[:, :], routed[:, 0, :], start=True, stop=True)
            mm(ps[:, TB, 8:16], ones[:, :], routed[:, 0, :], start=True, stop=False)
            mm(ps[:, TB, 8:16], before[:, :], routed[:, 1, :], start=False, stop=True)
            mm(ps[:, TB, 16:24], ones[:, :], routed[:, 0, :], start=True, stop=False)
            mm(ps[:, TB, 16:24], ones[:, :], routed[:, 1, :], start=False, stop=True).then_inc(S("slots_filled"), 1)
            pe.wait_ge(S("flag_ready"), 1)
            first = pe.value_load(flag[0:1, 0:1], min_val=0, max_val=3)
            with pe.If(first > 2):
                gather(0, 2 * P)
            with pe.Else():
                gather(0, P)
            with pe.Fori(0, EXPERTS - 1) as e:
                kind = pe.value_load(flag[0:1, bass.ds(e, 1)], min_val=0, max_val=3)
                by_rows(pe, kind, lambda rows: expert(e, rows))
                then = pe.value_load(flag[0:1, bass.ds(e + 1, 1)], min_val=0, max_val=3)
                with pe.If(then > 2):
                    gather(e + 1, 2 * P)
                with pe.Else():
                    gather(e + 1, P)
                by_rows(pe, kind, lambda rows: scatter(e, rows))
            e = EXPERTS - 1
            kind = pe.value_load(flag[0:1, e:e + 1], min_val=0, max_val=3)
            by_rows(pe, kind, lambda rows: (expert(e, rows), scatter(e, rows, last=True)))

        @block.scalar
        def _(act):
            link = chain(act, "act_order")
            a_ = nc.scalar.activation

            def copy(o, i):
                return a_(o, i, ACT.Copy)

            def row(i):
                full(act, "row", i)
                b = bank("row", i)
                if i < MOD_SLOTS:
                    copy(mods[:, :, :].rearrange("p a n -> p (a n)")[:, i * MODW:(i + 1) * MODW], b[:, 0:MODW]
                         ).then_inc(emptied("row", i), 1)
                    return
                if i >= MOD_SLOTS + 4:
                    act.wait_ge(S(f"row_stored{i % 4}"), 16 * ((i - MOD_SLOTS) // 4))
                r = 32 * (i % 4)
                copy(rowst[r:r + 1, :], b[r:r + 1, 0:MODW]).then_inc(emptied("row", i), 1)

            def fill(steps):
                for what, i in steps:
                    if what == "row":
                        row(i)
                    else:
                        full(act, "part", i)
                        copy(partst[:, i % 2, :], bank("part", i)[:, 0:MODW]).then_inc(emptied("part", i), 1)

            def transposed(name, *tag):
                t = tag[-1]
                for kk in range(2):
                    job = (name, *tag, kk)
                    full(act, *job)
                    copy(uT[:, 4 * kk:4 * kk + 4, t * P:(t + 1) * P],
                         bank(*job).rearrange("p (k n) -> p k n", k=4)).then_inc(emptied(*job), 1)

            def mixer(l):
                if l == 0:
                    act.wait_ge(S("c_in"), 16)
                    a_(csil[:, :], ccol[:, :], ACT.Silu).then_inc(S("csil_done"), 1)
                else:
                    ln_root(2 * l - 1, 0)
                fill(row_steps(START[l], None, True)[0])
                transposed("uT", l, 0, 0)
                if l == 0:
                    act.wait_ge(S("angle_folded"), 1)
                    a_(sn[:, :, :], ang[:, :, :], ACT.Sin)
                    a_(cs[:, :, :], ang2[:, :, :], ACT.Sin).then_inc(S("angles"), 1)
                if l > 0:
                    ln_root(2 * l - 1, 1)
                else:
                    act.wait_ge(S("consts"), 1)
                for t in range(2):
                    if t == 1:
                        transposed("uT", l, 0, 1)
                    job = (f"A1_{t}", l)
                    full(act, *job)
                    copy(A1[:, t, :], bank(*job)[:, 0:312]).then_inc(emptied(*job), 1)
                job = ("iq", l)
                full(act, *job)
                copy(iqT, bank(*job).rearrange("p (b t) -> p b t", b=2)).then_inc(emptied(*job), 1)
                job = ("A2", l)
                full(act, *job)
                copy(A2[:, :, :], bank(*job)[:, 0:256].rearrange("p (b t) -> p b t", b=2)).then_inc(emptied(*job), 1)
                job = ("ik", l)
                full(act, *job)
                copy(ik2[0:64, :], bank(*job)[0:64, 0:T])
                copy(ik2[64:128, :], bank(*job)[0:64, 0:T]).then_inc(emptied(*job), 1)
                job = ("qn", l)
                full(act, *job)
                copy(qnT, bank(*job).rearrange("p (b t) -> p b t", b=2)).then_inc(emptied(*job), 1)
                job = ("nq", l)
                full(act, *job)
                copy(nqT, bank(*job).rearrange("p (b t) -> p b t", b=2)).then_inc(emptied(*job), 1)
                act.wait_ge(S("kvss"), l + 1)
                a_(kvs[:, 2:4], kvs[:, 0:2], ACT.Sqrt, scale=1.0 / D_C, bias=eps6[:, :]).then_inc(S("kvrms"), 1)
                job = ("gT", l)
                full(act, *job)
                act.wait_ge(S("small_in"), 64 * (l + 1))
                b = bank(*job)
                a_(gi[:, :], b[0:4, 0:T], ACT.Identity, bias=gbt[:, 0:1])
                a_(gf[:, :], b[0:4, T:2 * T], ACT.Identity, bias=gbt[:, 1:2]).then_inc(emptied(*job), 1)
                copied(act, *job)
                link(a_(lse[:, :], gf[:, :], ACT.Abs))
                link(a_(lse[:, :], lse[:, :], ACT.Exp, scale=-1.0))
                a_(lse[:, :], lse[:, :], ACT.Ln, bias=1.0).then_inc(S("lse_done"), 1)

                def mqk(i):
                    job = (f"mqk{i}", l)
                    full(act, *job)
                    if i == 0:
                        act.wait_ge(S("raw_padded"), l + 1)
                    copy(rawv[:, 2 * i:2 * i + 2, 3:3 + T], bank(*job).rearrange("p (b t) -> p b t", b=2)
                         ).then_inc(emptied(*job), 1)

                def relus(t):
                    for odd, name in enumerate(("lgE", "lgO")):
                        job = (f"{name}{t}", l)
                        full(act, *job)
                        if odd == 0 and t == 1:
                            act.wait_ge(S("rel_used"), 2 * l + 1)
                        n = (t + 1) * P
                        a_(rel[:, odd:odd + 3:2, 0:n], bank(*job).rearrange("p (b t) -> p b t", b=2)[:, :, 0:n],
                           ACT.Relu).then_inc(emptied(*job), 1)
                mqk(0)
                mqk(1)
                relus(0)
                relus(1)
                mqk(2)
                mqk(3)
                job = ("ropeT", l)
                full(act, *job)
                b = bank(*job)
                for h in range(HEADS):
                    copy(ropeT[64 * (h % 2):64 * (h % 2) + 32, h // 2, :], b[32 * h:32 * h + 32, 0:T])
                copy(ropeT[0:32, 2, :], b[0:32, T:2 * T])
                copy(ropeT[64:96, 2, :], b[64:96, T:2 * T]).then_inc(emptied(*job), 1)
                job = ("ckvT", l)
                full(act, *job)
                copy(ckvT[:, :], bank(*job)[:, 0:T]).then_inc(emptied(*job), 1)

                def conv_silus(*blocks):
                    for b in blocks:
                        act.wait_ge(S("conv_sum"), 8 * l + b + 1)
                        a_(rawv[:, b, 3:3 + T], ct[:, b % 2, :], ACT.Silu).then_inc(S("conv_done"), 1)

                for t in range(2):
                    job = (f"mv{t}", l)
                    full(act, *job)
                    copy(mvt[:, t, 0:3, 0:DH_B], bank(*job)[:, 0:384].rearrange("p (h d) -> p h d", h=3)
                         ).then_inc(emptied(*job), 1)
                    if t == 1:
                        conv_silus(0, 1)
                for t in range(2):
                    job = (f"vo{t}", l)
                    full(act, *job)
                    copy(mvt[:, t, 3, 0:DH_B], bank(*job)[:, 0:P])
                    a_(mog[:, t, 0:256], bank(*job)[:, P:384], ACT.Sigmoid).then_inc(emptied(*job), 1)
                    conv_silus(2 * t + 2, 2 * t + 3)
                job = ("mo", l)
                full(act, *job)
                a_(mog[:, :, 256:512], bank(*job).rearrange("p (t n) -> p t n", t=2), ACT.Sigmoid
                   ).then_inc(emptied(*job), 1)
                a_(gates[:, :, :], A1[:, :, 300:312], ACT.Sigmoid).then_inc(S("gates_ready"), 1)
                job = ("cmpp", l)
                full(act, *job)
                copy(cmps, bank(*job)[:, 0:2 * P]).then_inc(emptied(*job), 1)
                for odd, name in enumerate(("qabsE", "qabsO")):
                    job = (name, l)
                    full(act, *job)
                    copy(qabsT[:, odd:odd + 3:2, :], bank(*job).rearrange("p (b t) -> p b t", b=2)
                         ).then_inc(emptied(*job), 1)
                conv_silus(6, 7)
                job = ("cmph", l)
                full(act, *job)
                a_(hid[:, :, :], bank(*job)[:, 0:2 * N_CMP].rearrange("p (j n) -> p j n", j=2), ACT.Silu
                   ).then_inc(emptied(*job), 1)
                job = ("cmpkv", l)
                full(act, *job)
                b = bank(*job)
                copy(kcmp[0:64, 0, :], b[0:64, 0:N_CMP])
                copy(kcmp[64:128, 1, :], b[0:64, 0:N_CMP])
                for h in range(HEADS):
                    ins = copy(vbd[32 * h:32 * h + N_CMP, h, :], b[0:N_CMP, 64:128])
                ins.then_inc(emptied(*job), 1)
                act.wait_ge(S("Pc_shifted"), l + 1)
                a_(Pc[:, :, :, 0:N_CMP], Pc[:, :, :, 0:N_CMP], ACT.Exp, scale=SCALE_C).then_inc(S("Pc_exp"), 1)

                def exps(n):
                    kind, t = UNITS[n]
                    m = (t + 1) * P
                    sc = SCALE_A if kind == "A" else SCALE_C
                    act.wait_ge(S("prob_ready"), 6 * l + n + 1)
                    for h in range(HEADS):
                        ins = a_(prob[:, n % 2, h, 0:m], prob[:, n % 2, h, 0:m], ACT.Exp, scale=sc,
                                 bias=mx[:, n, h:h + 1], accum_out=rs[:, n, h:h + 1])
                    ins.then_inc(S("exp_done"), 1)

                def turned(n):
                    kind, t = UNITS[n]
                    for kb in range(t + 1):
                        job = ("PT", l, n, kb)
                        full(act, *job)
                        if kb == 0 and n > 0:
                            full(act, "ol" if UNITS[n - 1][0] == "A" else "o", l, n - 1)
                        copy(PTs[:, kb, :], bank(*job)).then_inc(emptied(*job), 1)
                    if kind == "A":
                        job = ("ol", l, n)
                        full(act, *job)
                        copy(olT, bank(*job).rearrange("p (h t) -> p h t", h=4)).then_inc(emptied(*job), 1)

                for n in range(len(UNITS) + 1):
                    if n < len(UNITS):
                        fill(fill_steps(l)[n])
                    if n == 0:
                        job = ("PcT", l)
                        full(act, *job)
                        copy(PcT[:, :], bank(*job)[:, 0:T]).then_inc(emptied(*job), 1)
                    if n < len(UNITS) and n == 0:
                        exps(0)
                    if n >= 1:
                        turned(n - 1)
                        if n < len(UNITS):
                            exps(n)
                job = ("cT", l)
                full(act, *job)
                copy(ccl[:, :], bank(*job)[:, 0:8])
                a_(emc[:, :], bank(*job)[:, 8:16], ACT.Exp, scale=-1.0).then_inc(emptied(*job), 1)
                copied(act, "cT", l)
                copied(act, "Mb1", l)
                for h in range(HEADS):
                    a_(Dm[:, h, 0:T], Dm[:, h, 0:T], ACT.Exp, bias=ccl[:, h:h + 1])
                    a_(Dm[:, h, T:T + P], Dm[:, h, T:T + P], ACT.Exp, bias=ccl[:, 4 + h:5 + h]
                       ).then_inc(S("Dm_exp"), 1)
                act.wait_ge(S("ss_ready"), 3 * l + 1)
                a_(rstd[:, :, 0:8], ss[:, :, 0:8], ACT.Sqrt, scale=1.0 / 64, bias=eps6[:, :]
                   ).then_inc(S("rms_ready"), 1)
                fill(fill_steps(l)[6])

                def rms_root(t):
                    act.wait_ge(S("ss_ready"), 3 * l + t + 2)
                    a_(rstd[:, t, 8:12], ss[:, t, 8:12], ACT.Sqrt, scale=1.0 / DH_B, bias=eps6[:, :]
                       ).then_inc(S("rms_ready"), 1)
                rms_root(0)
                fill(fill_steps(l)[7])
                transposed("yT", l, 0)
                rms_root(1)
                transposed("yT", l, 1)
                for t in range(2):
                    ln_root(2 * l, t)
                    transposed("uT", l, 1, t)

            def ln_root(half, t):
                act.wait_ge(S("var_ready"), 2 * half + t + 1)
                a_(lsd[:, t:t + 1], mv2[:, t, 1:2], ACT.Sqrt, bias=eps5[:, :]).then_inc(S("std_ready"), 1)

            def swiglu(rows, chunks, first, after_first=None):
                blocks = rows // P
                for c in range(chunks + 1):
                    if c > 0:
                        act.wait_ge(S("hT_filled"), first + c)
                        if rows < P:
                            ins = copy(hT[:, 0, 0, :], ps[:, TB, 0:P])
                            if rows == 96:
                                b = ps[0:64, TB, P:2 * P].rearrange("p (b a s) -> p b a s", b=2, a=2)
                                for a in range(2):
                                    ins = copy(hT[64 * a:64 * a + 64, 1, :, 0:32], b[:, :, a, :])
                        else:
                            ins = copy(hT[:, 0:blocks, :, :],
                                       ps[:, TB, 0:blocks * 256].rearrange("p (j b s) -> p j b s", j=blocks, b=2))
                        ins.then_inc(S("hT_ready"), 1)
                    if c < chunks:
                        act.wait_ge(S("gu_filled"), first + c + 1)
                        if rows < P:
                            ins = a_(sgb[:, 0, 0:P], ps[:, GU, 0:P], ACT.Silu)
                            if rows == 96:
                                ins = a_(sgb[:, 1, 0:64], ps[:, GU + 1, 0:64], ACT.Silu)
                        else:
                            ins = a_(sgb[:, 0:blocks, :], ps[:, GU:GU + blocks, 0:FC], ACT.Silu)
                        ins.then_inc(S("silu_done"), 1)
                        if c == 0 and after_first:
                            after_first()

            def gathered(e, n):
                for kp in range(4):
                    act.wait_ge(S("gather_filled"), 4 * e + kp + 1)
                    copy(uT[:, 2 * kp:2 * kp + 2, 0:n],
                         ps[:, kp, :].rearrange("p (i s) -> p i s", i=2)[:, :, 0:n]).then_inc(S("gather_ready"), 1)

            def expert(e, rows):
                def turned_weights():
                    act.wait_ge(S("gwT_filled"), e + 1)
                    if rows < P:
                        for a in (0, 64):
                            ins = copy(gwT[a:a + 64, 0, :], ps[0:64, XB, 0:T])
                        if rows == 96:
                            for a in range(0, P, 32):
                                ins = copy(gwT[a:a + 32, 1, :], ps[0:32, XB, T:2 * T])
                    else:
                        for j in range(rows // P):
                            ins = copy(gwT[:, j, :], ps[:, XB, j * T:(j + 1) * T])
                    ins.then_inc(S("gwT_ready"), 1)

                swiglu(rows, C_EXP, C_EXP * e + C_DENSE, turned_weights)
                act.wait_ge(S("down_done"), C_EXP * (e + 1) + C_DENSE)
                for i in range({2 * P: 4, 96: 3}.get(rows, 2)):
                    ins = copy(oe[:, i // 2, (i % 2) * 512:(i % 2 + 1) * 512], ps[:, ACC + i, :])
                ins.then_inc(S("oe_ready"), 1)

            act.wait_ge(S("eps_ready"), 1)
            mixer(0)
            swiglu(2 * P, C_DENSE, 0)
            mixer(1)
            act.wait_ge(S("gap_ready"), 1)
            a_(w12[:, :, 1], w12[:, :, 0], ACT.Exp).then_inc(S("gap_exp"), 1)
            act.wait_ge(S("flag_ready"), 1)
            first = act.value_load(flag[0:1, 0:1], min_val=0, max_val=3)
            with act.If(first > 2):
                gathered(0, 2 * P)
            with act.Else():
                gathered(0, P)
            with act.Fori(0, EXPERTS - 1) as e:
                kind = act.value_load(flag[0:1, bass.ds(e, 1)], min_val=0, max_val=3)
                by_rows(act, kind, lambda rows: expert(e, rows))
                then = act.value_load(flag[0:1, bass.ds(e + 1, 1)], min_val=0, max_val=3)
                with act.If(then > 2):
                    gathered(e + 1, 2 * P)
                with act.Else():
                    gathered(e + 1, P)
            e = EXPERTS - 1
            kind = act.value_load(flag[0:1, e:e + 1], min_val=0, max_val=3)
            by_rows(act, kind, lambda rows: expert(e, rows))
            for t in range(2):
                ln_root(3, t)

        @block.vector
        def _(dve):
            link = chain(dve, "dve_order")
            v = nc.vector
            tt, tsc, stt = v.tensor_tensor, v.tensor_scalar, v.scalar_tensor_tensor

            v.memset(eps5[:, :], 1e-5)
            v.memset(eps6[:, :], 1e-6).then_inc(S("eps_ready"), 1)

            def modulate(half, t):
                dve.wait_ge(S("modss_in"), 16 * half)
                link(stt(u[:, t, :], modss[:, 1, :], 1.0, x[:, t, :], ALU.add, ALU.mult))
                tt(u[:, t, :], u[:, t, :], modss[:, 0, :], ALU.add).then_inc(S("u_done"), 1)

            def first_modulate():
                dve.wait_ge(S("x_in"), 16)
                c0 = 4 * MODW - D
                for row, c in ((3, slice(0, c0)), (5, slice(c0, D))):
                    copied(dve, "row", row)
                    for t in range(TILES):
                        link(stt(u[:, t, c], modss[:, 1, c], 1.0, x[:, t, c], ALU.add, ALU.mult))
                        ins = tt(u[:, t, c], u[:, t, c], modss[:, 0, c], ALU.add)
                        if row == 5:
                            ins.then_inc(S("u_done"), 1)

            def angles():
                dve.wait_ge(S("pos_in"), 32)
                link(v.tensor_copy(lsd[:, :], pos[:, :]))
                for t in range(TILES):
                    ins = tsc(ang[:, t, :], freq[:, :], lsd[:, t:t + 1], None, ALU.mult)
                link(ins)
                link(tsc(ang2[:, :, :], ang[:, :, :], 1.0 / TWO_PI, None, ALU.mult))
                link(tsc(ang2[:, :, :], ang2[:, :, :], 12582912.0, None, ALU.add))
                link(tsc(ang2[:, :, :], ang2[:, :, :], -12582912.0, None, ALU.add))
                for part in PI_PARTS:
                    link(stt(ang[:, :, :], ang2[:, :, :], -part, ang[:, :, :], ALU.mult, ALU.add))
                link(tsc(ang[:, :, :], ang[:, :, :], PI_IN, -PI_IN, ALU.min, ALU.max))
                link(stt(ang2[:, :, :], ang[:, :, :], -1.0, ang[:, :, :], ALU.mult, ALU.max))
                tsc(ang2[:, :, :], ang2[:, :, :], -1.0, float(np.pi / 2), ALU.mult, ALU.add
                    ).then_inc(S("angle_folded"), 1)

            def add_norm(half, t, parts):
                if half:
                    dve.wait_ge(S("modg_in"), 16 * half)
                else:
                    copied(dve, "row", 7)
                for h, (wait, y, give) in enumerate(parts):
                    wait()
                    c = slice(h * 512, (h + 1) * 512)
                    ins = stt(u[:, t, c], modg[:, c], 1.0, y, ALU.add, ALU.mult)
                    if give is not None:
                        ins.then_inc(give, 1)
                if give is None:
                    link(ins)
                else:
                    copied(dve, "out", half // 2, t, 1)
                stt(x[:, t, :], x[:, t, :], ALPHA, u[:, t, :], ALU.mult, ALU.add).then_inc(S("z_done"), 1)
                n = 2 * half + t + 1
                dve.wait_ge(S("z_done"), n)
                for h in range(2):
                    ins = v.bn_stats(bst[:, t, h, :], x[:, t, h * 512:(h + 1) * 512])
                link(ins)
                v.bn_aggr(mv2[:, t, :], bst[:, t, :, :]).then_inc(S("var_ready"), 1)
                dve.wait_ge(S("ln_in"), 16 * (half + 1))
                dve.wait_ge(S("var_ready"), n)
                link(stt(x[:, t, :], x[:, t, :], mv2[:, t, 0:1], lnp[:, 0, :], ALU.subtract, ALU.mult))
                dve.wait_ge(S("std_ready"), n)
                link(v.reciprocal(lsd[:, t:t + 1], lsd[:, t:t + 1]))
                stt(x[:, t, :], x[:, t, :], lsd[:, t:t + 1], lnp[:, 1, :], ALU.mult, ALU.add
                    ).then_inc(S("x_done"), 1)
                dve.wait_ge(S("x_done"), n)

            def per_head(a, n, w):
                return a.unsqueeze(2).broadcast_to([P, n, w])

            def mixer(l):
                if l == 0:
                    first_modulate()
                    angles()
                if l == 0:
                    dve.wait_ge(S("consts"), 1)
                copied(dve, "A1_1", l)
                dve.wait_ge(S("small_in"), 64 * (l + 1))
                for t in range(TILES):
                    c = A1[:, t, 160:288]
                    ins = stt(ckvn[:, t, :], c, 1.0, c, ALU.mult, ALU.mult, accum_out=kvs[:, t:t + 1])
                ins.then_inc(S("kvss"), 1)
                job = ("kv", l)
                full(dve, *job)
                b = bank(*job)
                for j, r in enumerate((slice(0, 64), slice(64, 128))):
                    v.tensor_copy(kc2[0:64, j, :], b[r, 0:T])
                    v.tensor_copy(kc2[64:128, j, 0:T - 1], b[r, 1:T])
                for dst, r in ((ks2, slice(0, 64)), (kw2, slice(64, 128))):
                    v.tensor_copy(dst[0:64, :], b[r, T:2 * T])
                    ins = v.tensor_copy(dst[64:128, :], b[r, T:2 * T])
                ins.then_inc(emptied(*job), 1)
                copied(dve, *job)
                for j in range(2):
                    src = kc2[:, j, :]
                    win = bass.AP(src.tensor, src.offset, [list(src.ap[0]), [2, 16], [16, N_CMP]])
                    pe_ = lw[:, LW_POS + 16 * j:LW_POS + 16 * (j + 1)].unsqueeze(2).broadcast_to([P, 16, N_CMP])
                    ins = tt(blocks[:, j, :, :], win, pe_, ALU.add)
                ins.then_inc(S("blk_done"), 1)
                dve.wait_ge(S("kvrms"), l + 1)
                link(v.reciprocal(kvs[:, 2:4], kvs[:, 2:4]))
                for t in range(TILES):
                    ins = stt(ckvn[:, t, :], A1[:, t, 160:288], kvs[:, 2 + t:3 + t], kvn[:, :], ALU.mult, ALU.mult)
                ins.then_inc(S("ckvn_done"), 1)
                for t in range(TILES):
                    n = (t + 1) * P
                    s = score[:, t, 0:n]
                    copied(dve, f"lgO{t}", l)
                    for h in range(HEADS):
                        ins = stt(s, rel[:, h, 0:n], A1[:, t, 288 + h:289 + h], cm[:, T - n:T] if h == 0 else s,
                                  ALU.mult, ALU.add)
                        if h < HEADS - 1:
                            link(ins)
                    ins.then_inc(S("rel_used"), 1)
                    dve.wait_ge(S("rel_used"), 2 * l + t + 1)
                    for _ in range(K_SEL // 8):
                        link(v.max(max8[:, :], s))
                        link(v.match_replace(s, max8[:, :], s, TAKEN))
                    link(tsc(s, s, TAKEN / 2, NEG, ALU.is_gt, ALU.mult))
                    link(tt(s, s, cm[:, T - n:T], ALU.add))
                for b in range(8):
                    copied(dve, f"mqk{b // 2}", l)
                    if b >= 2 or l > 0:
                        dve.wait_ge(S("conv_done"), 8 * l + b - 1 if b >= 2 else 8 * l)
                    o = ct[:, b % 2, :]
                    cw = LW_CW + 4 * b
                    link(tsc(o, rawv[:, b, 0:T], lw[:, cw:cw + 1], lw[:, LW_CB + b:LW_CB + b + 1], ALU.mult, ALU.add))
                    for j in range(1, 4):
                        ins = stt(o, rawv[:, b, j:j + T], lw[:, cw + j:cw + j + 1], o, ALU.mult, ALU.add)
                        if j < 3:
                            link(ins)
                    ins.then_inc(S("conv_sum"), 1)
                dve.wait_ge(S("sums_done"), l + 1)
                src, dst = scanB, scanA
                for d in SHIFTS:
                    link(tt(dst[:, P:P + T], src[:, P:P + T], src[:, P - d:P + T - d], ALU.max))
                    src, dst = dst, src
                tt(brow[:, :], brow[:, :], scanB[:, P:P + T], ALU.add).then_inc(S("scans_done"), 1)
                pc = Pc[:, :, :, 0:N_CMP]
                full(dve, "cS", l)
                tt(pc, bank("cS", l)[:, 0:8 * N_CMP].rearrange("p (t h n) -> p t h n", t=2, h=4),
                   cmpa[:, :, :].unsqueeze(2).broadcast_to([P, TILES, HEADS, N_CMP]), ALU.add
                   ).then_inc(emptied("cS", l), 1)
                copied(dve, "cS", l)
                link(v.tensor_reduce(st8[:, :, :], pc, X, ALU.max))
                tt(pc, pc, st8[:, :, :].unsqueeze(3).broadcast_to([P, TILES, HEADS, N_CMP]), ALU.subtract
                   ).then_inc(S("Pc_shifted"), 1)
                dve.wait_ge(S("Pc_exp"), l + 1)
                link(tt(pc, pc, cmpm[:, :, :].unsqueeze(2).broadcast_to([P, TILES, HEADS, N_CMP]), ALU.mult))
                link(v.tensor_reduce(st8[:, :, :], pc, X, ALU.add))
                link(tsc(st8[:, :, :], st8[:, :, :], 1e-30, None, ALU.max))
                link(v.reciprocal(st8[:, :, :], st8[:, :, :]))
                tt(pc, pc, st8[:, :, :].unsqueeze(3).broadcast_to([P, TILES, HEADS, N_CMP]), ALU.mult
                   ).then_inc(S("Pc_done"), 1)
                dve.wait_ge(S("gates_ready"), l + 1)
                dve.wait_ge(S("conv_done"), 8 * (l + 1))

                def probs(n):
                    kind, t = UNITS[n]
                    m = (t + 1) * P
                    if n >= 2:
                        full(dve, "PT", l, n - 2, UNITS[n - 2][1])
                    mask = score[:, t, 0:m] if kind == "A" else cm[:, T - m:T]
                    for part in range(2):
                        job = ("sc", l, n, part)
                        full(dve, *job)
                        ins = tt(prob[:, n % 2, 2 * part:2 * part + 2, 0:m],
                                 bank(*job).rearrange("p (i t) -> p i t", i=2)[:, :, 0:m],
                                 mask.unsqueeze(1).broadcast_to([P, 2, m]), ALU.add)
                        ins.then_inc(emptied(*job), 1)
                    copied(dve, *job)
                    link(v.tensor_reduce(mx[:, n, :], prob[:, n % 2, :, 0:m], X, ALU.max))
                    tsc(mx[:, n, :], mx[:, n, :], -(SCALE_A if kind == "A" else SCALE_C), None, ALU.mult
                        ).then_inc(S("prob_ready"), 1)

                def outputs(n):
                    kind, t = UNITS[n]
                    dve.wait_ge(S("exp_done"), 6 * l + n + 1)
                    link(v.reciprocal(rs[:, n, :], rs[:, n, :]))
                    if kind != "A":
                        g = gates[:, t, 4:8] if kind == "S" else gates[:, t, 8:12]
                        for part in range(2):
                            ins = tt(mx[:, n, part:part + 3:2], rs[:, n, 2 * part:2 * part + 2], g[:, part:part + 3:2],
                                     ALU.mult)
                        link(ins)
                    job = ("o", l, n)
                    full(dve, *job)
                    o = bank(*job)[:, 0:256].rearrange("p (h d) -> p h d", h=4)
                    if kind == "A":
                        for part in range(2):
                            ins = tt(u[:, t, 0:256].rearrange("p (h d) -> p h d", h=4)[:, part:part + 3:2, :],
                                     o[:, 2 * part:2 * part + 2, :],
                                     per_head(rs[:, n, 2 * part:2 * part + 2], 2, 64), ALU.mult)
                        ins.then_inc(emptied(*job), 1)
                        copied(dve, *job)
                    else:
                        tmp = ct[:, 0, :].rearrange("p (h d) -> p h d", h=4)
                        y = u[:, t, 768:1024].rearrange("p (h d) -> p h d", h=4)
                        tt(tmp, o, per_head(mx[:, n, :], 4, 64), ALU.mult).then_inc(emptied(*job), 1)
                        copied(dve, *job)
                        link(tt(y, y, tmp, ALU.add))

                for n in range(len(UNITS) + 1):
                    if n < len(UNITS):
                        probs(n)
                    if n == 0:
                        job = ("oC", l)
                        full(dve, *job)
                        for t in range(TILES):
                            ins = tt(u[:, t, 768:1024].rearrange("p (h d) -> p h d", h=4),
                                     bank(*job)[:, t * 256:(t + 1) * 256].rearrange("p (h d) -> p h d", h=4),
                                     per_head(gates[:, t, 0:4], 4, 64), ALU.mult)
                        ins.then_inc(emptied(*job), 1)
                        copied(dve, *job)
                    if n >= 1:
                        outputs(n - 1)

                for p in range(2):
                    job = (f"Mb{p}", l)
                    full(dve, *job)
                    b = bank(*job).rearrange("p (i t) -> p i t", i=2)
                    stt(Dm[:, 2 * p:2 * p + 2, 0:T], b, -1.0, cmT[:, :].unsqueeze(1).broadcast_to([P, 2, T]),
                        ALU.mult, ALU.add)
                    ins = stt(Dm[:, 2 * p:2 * p + 2, T:T + P], b[:, :, P:T], -1.0,
                              cmT[:, 0:P].unsqueeze(1).broadcast_to([P, 2, P]), ALU.mult, ALU.add)
                    ins.then_inc(emptied(*job), 1)
                sq = prob[:, :, :, :].rearrange("p a h t -> p a (h t)")
                groups = ((slice(0, 256), slice(0, 4)), (slice(768, 1024), slice(4, 8)))
                for c, _ in groups:
                    ins = tt(sq[:, :, c], u[:, :, c], u[:, :, c], ALU.mult)
                link(ins)
                for c, g in groups:
                    ins = v.tensor_reduce(ss[:, :, g], sq[:, :, c].rearrange("p a (g d) -> p a g d", d=64), X, ALU.add)
                ins.then_inc(S("ss_ready"), 1)
                for h in range(HEADS):
                    job = ("sM", l, h)
                    full(dve, *job)
                    dve.wait_ge(S("Dm_exp"), 4 * l + h + 1)
                    stt(Dm[:, h, :], bank(*job)[:, 0:384], SCALE_B, Dm[:, h, :], ALU.mult, ALU.mult
                        ).then_inc(emptied(*job), 1)
                dve.wait_ge(S("rms_ready"), 3 * l + 1)
                link(v.reciprocal(rstd[:, :, 0:8], rstd[:, :, 0:8]))
                for c, g in groups:
                    for t in range(TILES):
                        y4 = u[:, t, c].rearrange("p (g d) -> p g d", d=64)
                        ins = tt(y4, y4, per_head(rstd[:, t, g], 4, 64), ALU.mult)
                link(ins)
                for c, _ in groups:
                    ins = tt(u[:, :, c], u[:, :, c], gn[:, c].unsqueeze(1).broadcast_to([P, TILES, 256]), ALU.mult)
                link(ins)
                link(tt(mog[:, :, :], mog[:, :, :], gn[:, 256:768].unsqueeze(1).broadcast_to([P, TILES, 512]),
                        ALU.mult))
                copied(dve, "cT", l)

                def hidden(t):
                    for p in range(2):
                        job = ("hM", l, t, p)
                        full(dve, *job)
                        b = bank(*job)[:, 0:258].rearrange("p (i d) -> p i d", i=2)
                        link(v.tensor_copy(dn[:, 0:2], b[:, :, 128]))
                        link(stt(dn[:, 2:4], dn[:, 0:2], -1.0, dn[:, 0:2], ALU.mult, ALU.max))
                        link(tt(dn[:, 2:4], dn[:, 2:4], emc[:, 4 * t + 2 * p:4 * t + 2 * p + 2], ALU.max))
                        link(v.reciprocal(dn[:, 2:4], dn[:, 2:4]))
                        ins = tt(u[:, t, 256 + 256 * p:512 + 256 * p].rearrange("p (i d) -> p i d", i=2), b[:, :, 0:128],
                                 per_head(dn[:, 2:4], 2, 128), ALU.mult)
                        ins.then_inc(emptied(*job), 1)
                        copied(dve, *job)

                def rms_mlstm(t):
                    y, q = u[:, t, 256:768], sq[:, t, 256:768]
                    link(tt(q, y, y, ALU.mult))
                    v.tensor_reduce(ss[:, t, 8:12], q.rearrange("p (g d) -> p g d", d=DH_B), X, ALU.add
                                    ).then_inc(S("ss_ready"), 1)
                    dve.wait_ge(S("rms_ready"), 3 * l + t + 2)
                    link(v.reciprocal(rstd[:, t, 8:12], rstd[:, t, 8:12]))
                    y4 = y.rearrange("p (g d) -> p g d", d=DH_B)
                    link(tt(y4, y4, per_head(rstd[:, t, 8:12], 4, DH_B), ALU.mult))
                    tt(y, y, mog[:, t, :], ALU.mult).then_inc(S("y_done"), 1)

                for t in range(TILES):
                    hidden(t)
                    rms_mlstm(t)
                for t in range(TILES):
                    parts = []
                    for h in range(2):
                        job = ("out", l, t, h)
                        parts.append(((lambda job=job: full(dve, *job)), bank(*job), emptied(*job)))
                    add_norm(2 * l, t, parts)
                    modulate(2 * l + 1, t)

            def swiglu(rows, chunks, first):
                blocks = rows // P
                for c in range(chunks):
                    dve.wait_ge(S("silu_done"), first + c + 1)
                    if rows < P:
                        ins = tt(hbuf[:, 0, 0:P], sgb[:, 0, 0:P], ps[:, GU, P:2 * P], ALU.mult)
                        if rows == 96:
                            ins = tt(hbuf[:, 1, 0:64], sgb[:, 1, 0:64], ps[:, GU + 1, 64:P], ALU.mult)
                    else:
                        ins = tt(hbuf[:, 0:blocks, :], sgb[:, 0:blocks, :], ps[:, GU:GU + blocks, FC:2 * FC], ALU.mult)
                    ins.then_inc(S("h_ready"), 1)

            def select(e):
                v.tensor_copy(now[:, :], table[:, :, bass.ds(e, 1)].rearrange("p a b -> p (a b)")
                              ).then_inc(S("now_ready"), 1)
                dve.wait_ge(S("now_ready"), e + 1)
                for t in range(TILES):
                    tsc(gsel[:, t, :], iota, now[:, t:t + 1], None, ALU.is_equal)
                for t in range(TILES):
                    ins = tsc(gwsel[:, t, :], iota, now[:, t:t + 1], now[:, 2 + t:3 + t], ALU.is_equal, ALU.mult)
                ins.then_inc(S("sel_ready"), 1)

            def add_up(e, t):
                for half in range(2):
                    i = 2 * t + half
                    dve.wait_ge(S("scatter_filled"), 4 * e + i + 1)
                    c = slice(half * 512, (half + 1) * 512)
                    tt(yacc[:, t, c], yacc[:, t, c], ps[:, i, :], ALU.add).then_inc(S("y_added"), 1)

            mixer(0)
            swiglu(2 * P, C_DENSE, 0)
            for t in range(TILES):
                def wait():
                    if t == 0:
                        dve.wait_ge(S("first_block_done"), 1)
                    else:
                        dve.wait_ge(S("down_done"), C_DENSE)
                add_norm(1, t, [(wait, ps[:, ACC + 2 * t + h, :], None) for h in range(2)])
                modulate(2, t)
            mixer(1)
            dve.wait_ge(S("logits_filled"), 1)
            link(v.tensor_copy(lg[:, :, :], ps[:, ACC, 0:16].rearrange("p (t e) -> p t e", t=2)))
            for t in range(TILES):
                link(v.max(top8[:, t, :], lg[:, t, :]))
                link(v.max_index(idx8[:, t, :], top8[:, t, :], lg[:, t, :]))
            v.tensor_copy(idxf[:, :, :], idx8[:, :, :])
            tt(w12[:, :, 0], top8[:, :, 1], top8[:, :, 0], ALU.subtract).then_inc(S("gap_ready"), 1)
            dve.wait_ge(S("gap_ready"), 1)
            dve.wait_ge(S("iota_ready"), 1)
            for k in range(2):
                for t in range(TILES):
                    ins = tsc(oh[:, k, t, :], iota[:, 0:EXPERTS], idxf[:, t, k:k + 1], None, ALU.is_equal)
            link(ins)
            tt(routed[:, :, :], oh[:, 0, :, :], oh[:, 1, :, :], ALU.add).then_inc(S("routed_done"), 1)
            dve.wait_ge(S("gap_exp"), 1)
            link(tsc(w12[:, :, 0], w12[:, :, 1], 1.0, None, ALU.add))
            link(v.reciprocal(w12[:, :, 0], w12[:, :, 0]))
            link(tt(w12[:, :, 1], w12[:, :, 1], w12[:, :, 0], ALU.mult))
            for t in range(TILES):
                ins = tsc(oh[:, 0, t, :], oh[:, 0, t, :], w12[:, t, 0:1], None, ALU.mult)
            link(ins)
            for t in range(TILES):
                ins = stt(table[:, 2 + t, :], oh[:, 1, t, :], w12[:, t, 1:2], oh[:, 0, t, :], ALU.mult, ALU.add)
            link(ins)
            dve.wait_ge(S("slots_filled"), 1)
            link(stt(table[:, 0:2, :], ps[:, TB, 0:16].rearrange("p (t e) -> p t e", t=2), 1.0, routed[:, :, :],
                     ALU.add, ALU.mult))
            link(tsc(table[:, 0:2, :], table[:, 0:2, :], -1.0, None, ALU.add))
            count = ps[0:1, TB, 16:24]
            link(tsc(lsd8[:, :], count, 64.0, None, ALU.is_gt))
            link(stt(lsd8[:, :], count, 96.0, lsd8[:, :], ALU.is_gt, ALU.add))
            stt(flag[:, :], count, 128.0, lsd8[:, :], ALU.is_gt, ALU.add).then_inc(S("flag_ready"), 1)
            dve.wait_ge(S("flag_ready"), 1)
            select(0)
            v.memset(yacc, 0.0).then_inc(S("y_added"), 1)
            with dve.Fori(0, EXPERTS - 1) as e:
                kind = dve.value_load(flag[0:1, bass.ds(e, 1)], min_val=0, max_val=3)
                by_rows(dve, kind, lambda rows: swiglu(rows, C_EXP, C_EXP * e + C_DENSE))
                select(e + 1)
                dve.wait_ge(S("y_added"), 4 * e + 1)
                for t in range(TILES):
                    add_up(e, t)
            e = EXPERTS - 1
            kind = dve.value_load(flag[0:1, e:e + 1], min_val=0, max_val=3)
            by_rows(dve, kind, lambda rows: swiglu(rows, C_EXP, C_EXP * e + C_DENSE))
            dve.wait_ge(S("y_added"), 4 * e + 1)
            for t in range(TILES):
                add_up(e, t)
                dve.wait_ge(S("y_added"), 4 * e + 2 * t + 3)
                add_norm(3, t, [((lambda: None), yacc[:, t, h * 512:(h + 1) * 512], None) for h in range(2)])


PI_1 = 6.28125
PI_2 = float(np.floor((TWO_PI - PI_1) * 2 ** 20) / 2 ** 20)
PI_PARTS = (PI_1, PI_2, TWO_PI - PI_1 - PI_2)
PI_IN = 3.1415925
BLOCKS = {nb: [(j, b) for j in range(nb) for b in range(2)] for nb in (1, 2)}
ORDER = (0, 2, 1, 3)
SHIFTS = [2 ** i for i in range(8)]


def pack(inputs):
    a = {k: np.asarray(v) for k, v in inputs.items()}
    L = DEPTH

    def swiglu(gate, up, down):
        n, f = gate.shape[0], gate.shape[2]
        c = f // FC
        out = np.empty((n, c, 2, P, SLOT), np.float32)
        gu = out[..., 0:2048].reshape(n, c, 2, P, 4, 2, FC)
        for j, w in enumerate((gate, up)):
            gu[:, :, :, :, :, j] = w.reshape(n, 2, 4, P, c, FC).transpose(0, 4, 1, 3, 2, 5)
        out[..., 0:2048] = gu.reshape(n, c, 2, P, 2048)
        out[..., 2048:] = down.reshape(n, c, 2, P, D)
        return out.reshape(n * c * 2, P, SLOT)

    cols = np.concatenate([OFF[n] + i + np.arange(w) for n, i, w in PICK])
    w = a["w_in"][:, :, cols].reshape(L, KD, P, -1)
    at, parts = 0, []
    for width in PROJ:
        parts.append(w[..., at:at + width].transpose(0, 2, 1, 3).reshape(L, -1))
        at += width
    w2, uk, uv = a["nsa_cmp_w2"], a["dsa_w_uk"], a["dsa_w_uv"]
    lw = [w2.transpose(0, 2, 1, 3).reshape(L, P, -1),
          uk.reshape(L, 2, 2, 64, D_C).transpose(0, 2, 3, 1, 4).reshape(L, P, -1),
          uv.transpose(0, 2, 1, 3).reshape(L, P, -1),
          a["mlstm_conv_w"].reshape(L, 4, 8, P).transpose(0, 3, 2, 1).reshape(L, P, -1),
          a["mlstm_conv_b"].reshape(L, 8, P).transpose(0, 2, 1),
          a["nsa_cmp_pos"].reshape(L, 2, 16, P).transpose(0, 3, 1, 2).reshape(L, P, -1)]
    return {
        "x": a["x"].reshape(T, D),
        "c": a["c"].reshape(KD, P).T,
        "positions": a["positions"].reshape(TILES, P).T,
        "inv_freq": np.float32(10000.0) ** (-np.arange(0, DH_R, 2, dtype=np.float32) / DH_R),
        "mod": a["w_mod"].reshape(KD, P, 32, MODW).transpose(2, 1, 0, 3).reshape(32, P, SLOT),
        "b_mod": a["b_mod"].reshape(32, MODW),
        "w_in": np.concatenate(parts, 1),
        "w1": a["nsa_cmp_w1"].reshape(L, 2, 16, P, P).transpose(0, 3, 1, 2, 4).reshape(L, P, -1),
        "lw": np.concatenate(lw, 2),
        "kv_norm": a["dsa_kv_norm"],
        "grp_norm": a["grp_norm"],
        "gate_b": a["mlstm_gate_b"].transpose(0, 2, 1),
        "ln": np.stack([a["ln_g"], a["ln_b"]], 2).reshape(2 * L, 2 * D),
        "w_out": a["w_out"].reshape(L, KD, P, D).transpose(0, 2, 1, 3).reshape(L, P, -1),
        "ffn": swiglu(a["ffn_w_gate"], a["ffn_w_up"], a["ffn_w_down"]),
        "router": a["moe_router"].reshape(KD, P, EXPERTS).transpose(1, 0, 2),
        "moe": swiglu(a["moe_w_gate"][0], a["moe_w_up"][0], a["moe_w_down"][0]),
    }


def kernel(**inputs):
    from concourse import bacc
    from concourse.bass_utils import run_bass_kernel_spmd

    nc = bacc.Bacc("TRN2", target_bir_lowering=False, num_devices=1)
    arrays, ins = {}, {}
    for name, a in pack(inputs).items():
        arrays[f"in_{name}"] = np.ascontiguousarray(a)
        ins[name] = nc.dram_tensor(f"in_{name}", a.shape, mybir.dt.from_np(a.dtype), kind="ExternalInput").ap()
    out = nc.dram_tensor("out_0", (T, D), F32, kind="ExternalOutput").ap()
    build_trunk(nc, ins, out)
    r = run_bass_kernel_spmd(nc, [arrays], core_ids=[0])
    return r.results[0]["out_0"].reshape(1, T, D)
```
